# Optimizing a Trainium2 kernel written in Bass

```python
import math
import jax, jax.numpy as jnp
from jax import lax
import numpy as np

D_MODEL = 2048
BATCH = 1
SEQ = 512
DEPTH = 1

D_HEAD = 64
N_ATTN_HEADS = D_MODEL // 256
D_VALUE = 2 * D_HEAD
ATTN_WIDTH = N_ATTN_HEADS * D_VALUE
CONV_WIDTH = D_MODEL // 2
CONV_SIZE = 3
Q_BLOCK = 128
ROPE_THETA = 10000.0
NORM_EPS = 1e-5
DEEPNORM_ALPHA = (2.0 * DEPTH) ** 0.25
DEEPNORM_BETA = (8.0 * DEPTH) ** -0.25
SEG_WIDTHS = (ATTN_WIDTH, ATTN_WIDTH, ATTN_WIDTH, ATTN_WIDTH,
              CONV_WIDTH, CONV_WIDTH, CONV_WIDTH, CONV_WIDTH,
              D_MODEL, D_MODEL)
IN_WIDTH = sum(SEG_WIDTHS)
SEG_SPLITS = tuple(int(v) for v in np.cumsum(SEG_WIDTHS)[:-1])

kernel_name = "hybrid_diffattn_shortconv_gated_deepnorm"

def _lambda_init(layer):
    return 0.8 - 0.6 * math.exp(-0.3 * layer)

def _rope_tables(positions):
    inv_freq = ROPE_THETA ** (-jnp.arange(0, D_HEAD, 2, dtype=jnp.float32) / D_HEAD)
    ang = positions.astype(jnp.float32)[..., None] * inv_freq
    return jnp.cos(ang)[:, :, None, None, :], jnp.sin(ang)[:, :, None, None, :]

def _apply_rope(t, cos, sin):
    t1, t2 = jnp.split(t.astype(jnp.float32), 2, axis=-1)
    return jnp.concatenate([t1 * cos - t2 * sin, t2 * cos + t1 * sin], axis=-1)

def _diff_attention(q, k, v, lam):
    B, S, H, _, dh = q.shape
    nb = S // Q_BLOCK
    vf = v.astype(jnp.float32)
    qb = (q * (dh ** -0.5)).reshape(B, nb, Q_BLOCK, H, 2, dh).transpose(1, 0, 2, 3, 4, 5)
    key_idx = jnp.arange(S, dtype=jnp.int32)

    def block(args):
        q_blk, start = args
        s = jnp.einsum('bqhmd,bkhmd->bhmqk', q_blk, k)
        q_idx = start + jnp.arange(Q_BLOCK, dtype=jnp.int32)
        causal = key_idx[None, :] <= q_idx[:, None]
        a = jax.nn.softmax(jnp.where(causal, s, -jnp.inf), axis=-1)
        p = a[:, :, 0] - lam * a[:, :, 1]
        return jnp.einsum('bhqk,bkhe->bqhe', p, vf)

    starts = jnp.arange(nb, dtype=jnp.int32) * Q_BLOCK
    o = lax.map(block, (qb, starts))
    return o.transpose(1, 0, 2, 3, 4).reshape(B, S, H, D_VALUE)

def _causal_dwconv(u, w):
    return lax.conv_general_dilated(
        u, w[:, None, :].astype(u.dtype), window_strides=(1,),
        padding=((CONV_SIZE - 1, 0),), dimension_numbers=('NWC', 'WIO', 'NWC'),
        feature_group_count=u.shape[-1])

def _layer(x, c, cos, sin, w_mod, b_mod, w_in, lq1, lk1, lq2, lk2, subln_gain,
           conv_w, w_proj_a, w_proj_b, w_out, ln_gain, ln_bias, lambda_init):
    B, S, D = x.shape
    mod = c @ w_mod + b_mod
    shift, scale, gate = jnp.split(mod, 3, axis=-1)
    u = x * (1.0 + scale[:, None, :]) + shift[:, None, :]

    proj = u @ w_in
    q, k, v, z_a, cb, cc, cx, z_b, g_a, g_b = jnp.split(proj, SEG_SPLITS, axis=-1)

    q = _apply_rope(q.reshape(B, S, N_ATTN_HEADS, 2, D_HEAD), cos, sin)
    k = _apply_rope(k.reshape(B, S, N_ATTN_HEADS, 2, D_HEAD), cos, sin)
    v = v.reshape(B, S, N_ATTN_HEADS, D_VALUE)
    lam = (jnp.exp(jnp.sum(lq1.astype(jnp.float32) * lk1.astype(jnp.float32)))
           - jnp.exp(jnp.sum(lq2.astype(jnp.float32) * lk2.astype(jnp.float32)))
           + lambda_init)
    o = _diff_attention(q, k, v, lam)
    o = o * lax.rsqrt(jnp.mean(o * o, axis=-1, keepdims=True) + NORM_EPS)
    o = o * subln_gain.astype(jnp.float32) * (1.0 - lambda_init)
    y_a = o.reshape(B, S, ATTN_WIDTH).astype(x.dtype) * jax.nn.silu(z_a)

    y_b = cb * _causal_dwconv(cc * cx, conv_w) * jax.nn.silu(z_b)

    h = jax.nn.sigmoid(g_a) * (y_a @ w_proj_a) + jax.nn.sigmoid(g_b) * (y_b @ w_proj_b)
    out = h @ w_out

    r = (DEEPNORM_ALPHA * x + gate[:, None, :] * out).astype(jnp.float32)
    mu = jnp.mean(r, axis=-1, keepdims=True)
    var = jnp.mean(jnp.square(r - mu), axis=-1, keepdims=True)
    y = (r - mu) * lax.rsqrt(var + NORM_EPS) * ln_gain.astype(jnp.float32) + ln_bias.astype(jnp.float32)
    return y.astype(x.dtype)

def setup_inputs(seed: int = 0) -> dict:
    key = jax.random.key(seed)
    ks = jax.random.split(key, 20)
    f32 = jnp.float32
    L, D = DEPTH, D_MODEL
    nrm = lambda k, shape: jax.random.normal(k, shape, f32)
    x = nrm(ks[0], (BATCH, SEQ, D))
    c = nrm(ks[1], (BATCH, D))
    positions = jnp.broadcast_to(jnp.arange(SEQ, dtype=jnp.int32), (BATCH, SEQ))
    w_mod = nrm(ks[2], (L, D, 3 * D)) * (0.2 * D ** -0.5)
    b_mod = nrm(ks[3], (L, 3 * D)) * 0.02
    col_scale = jnp.concatenate([
        jnp.full((w,), DEEPNORM_BETA if i in (2, 6) else 1.0, f32)
        for i, w in enumerate(SEG_WIDTHS)])
    w_in = nrm(ks[4], (L, D, IN_WIDTH)) * (D ** -0.5) * col_scale
    lq1 = nrm(ks[5], (L, D_HEAD)) * 0.1
    lk1 = nrm(ks[6], (L, D_HEAD)) * 0.1
    lq2 = nrm(ks[7], (L, D_HEAD)) * 0.1
    lk2 = nrm(ks[8], (L, D_HEAD)) * 0.1
    subln_gain = 1.0 + 0.02 * nrm(ks[9], (L, D_VALUE))
    conv_w = nrm(ks[10], (L, CONV_SIZE, CONV_WIDTH)) * (CONV_SIZE ** -0.5)
    w_proj_a = nrm(ks[11], (L, ATTN_WIDTH, D)) * (DEEPNORM_BETA * ATTN_WIDTH ** -0.5)
    w_proj_b = nrm(ks[12], (L, CONV_WIDTH, D)) * (DEEPNORM_BETA * CONV_WIDTH ** -0.5)
    w_out = nrm(ks[13], (L, D, D)) * (DEEPNORM_BETA * D ** -0.5)
    ln_gain = 1.0 + 0.02 * nrm(ks[14], (L, D))
    ln_bias = 0.02 * nrm(ks[15], (L, D))
    return {"x": x, "c": c, "positions": positions, "w_mod": w_mod, "b_mod": b_mod,
            "w_in": w_in, "lambda_q1": lq1, "lambda_k1": lk1, "lambda_q2": lq2,
            "lambda_k2": lk2, "subln_gain": subln_gain, "conv_w": conv_w,
            "w_proj_a": w_proj_a, "w_proj_b": w_proj_b, "w_out": w_out,
            "ln_gain": ln_gain, "ln_bias": ln_bias}

def reference(x, c, positions, w_mod, b_mod, w_in, lambda_q1, lambda_k1, lambda_q2,
              lambda_k2, subln_gain, conv_w, w_proj_a, w_proj_b, w_out, ln_gain, ln_bias):
    cos, sin = _rope_tables(positions)
    h = x
    for l in range(DEPTH):
        h = _layer(h, c, cos, sin, w_mod[l], b_mod[l], w_in[l], lambda_q1[l], lambda_k1[l],
                   lambda_q2[l], lambda_k2[l], subln_gain[l], conv_w[l], w_proj_a[l],
                   w_proj_b[l], w_out[l], ln_gain[l], ln_bias[l], _lambda_init(l))
    return h


_drawn_inputs = setup_inputs


def setup_inputs(seed=0):
    import zlib

    import numpy as np

    out = dict(_drawn_inputs(seed))
    spreads = {}
    factors = {'b_mod': 8.0,
     'lambda_q1': 200.0,
     'lambda_k1': 8.0,
     'lambda_q2': 8.0,
     'lambda_k2': 8.0,
     'subln_gain': 111.29,
     'conv_w': 4.026,
     'w_proj_a': 3.367,
     'w_proj_b': 4.109,
     'ln_gain': 21.425,
     'ln_bias': 21.331}
    for name, (base, spread) in spreads.items():
        noise = np.random.default_rng([zlib.crc32(name.encode()), seed]).standard_normal(out[name].shape)
        drawn = base * np.exp(spread * noise) if base else spread * noise
        out[name] = __import__('jax').numpy.asarray(drawn.astype(out[name].dtype))
    for name, factor in factors.items():
        out[name] = (out[name] * factor).astype(out[name].dtype)
    return out
```

```python
from contextlib import ExitStack

import numpy as np

import concourse.bass as bass
from concourse import mybir

F32 = mybir.dt.float32
F32R = mybir.dt.float32r
I32 = mybir.dt.int32
ALU = mybir.AluOpType
ACT = mybir.ActivationFunctionType
AX = mybir.AxisListType

P = 128
D = 2048
T = 512
KT = D // P
HEADS = 8
DH = 64
SEG = 1024
NT = T // P
COLS = 512
GATE_A, GATE_B = 8 * SEG, 8 * SEG + D
EPS = 1e-5
ALPHA = 2.0 ** 0.25
LAMBDA_INIT = 0.8 - 0.6
BIG = 3.0e38
RAW_START = 4
BASE = 1
LEAD = 3
SLOTS = 4

HC_HALVES, HC_BLOCKS = 16, 2
MERGE_HALVES, MERGE_BLOCKS = 12, 2
OUT_HALVES, OUT_BLOCKS = 8, 1
MERGES = D // COLS
A0, A_BLOCK0 = HEADS * HC_HALVES, HEADS * HC_BLOCKS
B0, B_BLOCK0 = A0 + MERGES * MERGE_HALVES, A_BLOCK0 + MERGES * MERGE_BLOCKS
O0, O_BLOCK0 = B0 + MERGES * MERGE_HALVES, B_BLOCK0 + MERGES * MERGE_BLOCKS
HALVES = O0 + (D // COLS) * OUT_HALVES

SCORE_AT = {3: (0, 0), 2: (1, 0), 0: (1, 384), 1: (2, 0)}
PROB_AT = {3: 0, 2: 512, 0: 896, 1: 1024}
PACKED = 1280

C_IDENT, C_MASK, C_MEAN, C_FREQ, C_SIGN, C_ONE, C_WIDTH = 0, 128, 256, 384, 385, 386, 387


def constants():
    c = np.zeros((P, C_WIDTH), np.float32)
    c[:, C_IDENT:C_IDENT + P] = np.eye(P)
    q, k = np.meshgrid(np.arange(P), np.arange(P), indexing="ij")
    c[:, C_MASK:C_MASK + P] = np.where(k <= q, BIG, -BIG)
    c[:, C_MEAN:C_MEAN + P] = 1.0 / P
    freq = (10000.0 ** (-np.arange(0, DH, 2) / DH)).astype(np.float32)
    c[:, C_FREQ] = np.tile(freq, 4)
    c[:, C_SIGN] = np.where((np.arange(P) // 32) % 2 == 0, -1.0, 1.0)
    c[:, C_ONE] = 1.0
    return c


def decoder_block(nc, x, xT, cT, positions, w_mod, b_mod, w_in, lams, gain, conv_w, w_tail,
                  ln_gain, ln_bias, consts, out):
    ctx = ExitStack()
    with ctx:
        def sb(name, shape, dt=F32, scope=None):
            return (scope or ctx).enter_context(nc.sbuf_tensor(name, shape, dt))

        def sem(name):
            return ctx.enter_context(nc.semaphore(name))

        raw = sb("raw", [P, 2, 4, COLS])
        w_hi = sb("w_hi", [P, SLOTS, 2, COLS], F32R)
        w_lo = sb("w_lo", [P, SLOTS, 2, COLS], F32R)
        act_hi = sb("act_hi", [P, KT, T], F32R)
        act_lo = sb("act_lo", [P, KT, T], F32R)
        gate = sb("gate", [P, D])
        cst = sb("cst", [P, C_WIDTH])
        cos = sb("cos", [P, T])
        sin = sb("sin", [P, T])
        c_col = sb("c_col", [P, KT])
        conv_col = sb("conv_col", [P, HEADS * 3])
        gain_col = sb("gain_col", [P, 1])
        eps_col = sb("eps_col", [P, 1])
        mod = sb("mod", [P, 2 * KT])
        lam_in = sb("lam_in", [P, 4, DH])
        lam_dot = sb("lam_dot", [P, 2])
        lam_exp = sb("lam_exp", [P, 2])
        neg_lam = sb("neg_lam", [P, 1])
        row_max = sb("row_max", [P, 4])
        neg_max = sb("neg_max", [P, 8])
        row_sum = sb("row_sum", [P, 8])
        stats = sb("stats", [P, NT, D // COLS, 6])
        mean_var = sb("mean_var", [P, NT, 2])
        rstd = sb("rstd", [P, NT])

        def stage(name_shapes):
            scope = ExitStack()
            made = [sb(n, s, d, scope) for n, s, d in name_shapes]
            scope.close()
            return made

        with ExitStack() as place:
            mod_sum = sb("mod_sum", [P, 2 * D], F32, place)
            place.close()
        with ExitStack() as place:
            sig_b = sb("sig_b", [P, 4, T], F32, place)
            place.close()
        ln_g, ln_b = stage([("ln_g", [P, D], F32), ("ln_b", [P, D], F32)])
        yb = sb("yb", [P, HEADS, T])
        x_in, w_mod_in = stage([("x_in", [P, KT, T], F32), ("w_mod_in", [P, 4, D], F32)])
        (ya, gate_in, q_raw, q_rot, k_raw, k_rot, q_f, k_f, v_f, v_tok, z_a, e_a, prob0, prob1,
         prob_t, o_f, prod, mix) = stage([
            ("ya", [P, HEADS, T], F32), ("gate_in", [P, D // 2], F32),
            ("q_raw", [P, T], F32), ("q_rot", [P, T], F32), ("k_raw", [P, T], F32),
            ("k_rot", [P, T], F32), ("q_f", [P, T], F32), ("k_f", [P, T], F32),
            ("v_f", [P, T], F32), ("v_tok", [P, T], F32), ("z_a", [P, T], F32),
            ("e_a", [P, T], F32), ("prob0", [P, PACKED], F32), ("prob1", [P, PACKED], F32),
            ("prob_t", [P, PACKED], F32), ("o_f", [P, T], F32), ("prod", [P, T + 2], F32),
            ("mix", [P, T], F32)])
        cb_f, cc_f = prob1[:, 0:T], prob1[:, T:2 * T]
        z_b, e_b, o_sq, rms = q_raw, q_rot, k_raw, k_rot
        h, y_hi, y_lo = stage([("h", [P, KT, T], F32), ("y_hi", [P, HEADS, T], F32R),
                               ("y_lo", [P, HEADS, T], F32R)])
        res, x_tok = stage([("res", [P, NT, D], F32), ("x_tok", [P, NT, D], F32)])

        acc = ctx.enter_context(nc.psum_tensor("acc", [P, 4, COLS], F32))
        sc = ctx.enter_context(nc.psum_tensor("sc", [P, 3, 512], F32))
        misc = ctx.enter_context(nc.psum_tensor("misc", [P, 512], F32))

        ident = cst[:, C_IDENT:C_IDENT + P]
        mask = cst[:, C_MASK:C_MASK + P]
        mean_mat = cst[:, C_MEAN:C_MEAN + P]
        one_col = cst[:, C_ONE:C_ONE + 1]

        small_in = sem("small_in")
        x_landed = sem("x_landed")
        bias_in = sem("bias_in")
        sums_clear = sem("sums_clear")
        mod_landed = [sem(f"mod_landed{s}") for s in range(4)]
        mod_free = sem("mod_free")
        mod_summed = sem("mod_summed")
        mod_reduced = sem("mod_reduced")
        lam_sem = sem("lam_sem")
        trig_ready = sem("trig_ready")
        sin_done = sem("sin_done")
        u_ready = sem("u_ready")
        u_hi_ready = sem("u_hi_ready")
        u_lo_ready = sem("u_lo_ready")
        raw_landed = [sem("raw_landed0"), sem("raw_landed1")]
        hi_ready = sem("hi_ready")
        lo_ready = sem("lo_ready")
        half_done = sem("half_done")
        bank_full = [sem(f"bank_full{n}") for n in range(3)]
        bank_drained = [sem(f"bank_drained{n}") for n in range(4)]
        gate_landed = sem("gate_landed")
        gate_free = sem("gate_free")
        gate_reduced = sem("gate_reduced")
        gate_ready = sem("gate_ready")
        qk_ready = sem("qk_ready")
        v_turned = sem("v_turned")
        v_ready = sem("v_ready")
        scores_done = sem("scores_done")
        max_ready = sem("max_ready")
        exp_done = sem("exp_done")
        p_ready = sem("p_ready")
        p_turned = sem("p_turned")
        pt_ready = sem("pt_ready")
        o_done = sem("o_done")
        o_drained = sem("o_drained")
        mean_done = sem("mean_done")
        rms_ready = sem("rms_ready")
        ya_done = sem("ya_done")
        yb_done = sem("yb_done")
        y_split = sem("y_split")
        h_ready = sem("h_ready")
        h_hi_ready = sem("h_hi_ready")
        h_split = sem("h_split")
        late_in = sem("late_in")
        step = sem("step")
        var_ready = sem("var_ready")
        std_ready = sem("std_ready")
        y_ready = sem("y_ready")
        stored = sem("stored")

        SMALL = 6
        block = ctx.enter_context(nc.Block())

        @block.sync
        def _(sp):
            sp.dma_start(c_col[:, :], cT).then_inc(small_in, 16)
            sp.dma_start(cst[:, :], consts).then_inc(small_in, 16)
            sp.dma_start(sin[:, :].bitcast(I32), positions.broadcast_to([P, T])).then_inc(small_in, 16)
            sp.dma_start(conv_col[:, :], conv_w).then_inc(small_in, 16)
            sp.dma_start(gain_col[:, :], gain).then_inc(small_in, 16)
            sp.dma_start(lam_in[:, :, :].rearrange("p a d -> p (a d)"),
                         lams.broadcast_to([P, 4 * DH])).then_inc(small_in, 16)
            for part, first_col in enumerate((D, 0)):
                with sp.Fori(0, KT // 4) as i:
                    for s in range(4):
                        sp.wait_ge(mod_free, i * 4 + (part * KT + s + 1))
                        sp.dma_start(w_mod_in[:, s, :],
                                     w_mod[bass.ds(i * (4 * P) + s * P, P), first_col:first_col + D]
                                     ).then_inc(mod_landed[s], 16)
            sp.dma_start(x_in[:, :, :], xT.rearrange("(k p) t -> p k t", p=P)).then_inc(x_landed, 16)

            def wait_raw(i, per, u):
                sp.wait_ge(lo_ready, i * (2 * per) + (2 * (u - 1) + RAW_START))

            with sp.Fori(0, HEADS) as i:
                for s in range(8):
                    base = 4 * SEG * (s // 4)
                    rows = w_in[(s % 4) * 4 * P:(s % 4 + 1) * 4 * P, base:base + 4 * SEG]
                    view = rows.rearrange("(k p) (g c) -> p k g c", p=P, g=4)
                    wait_raw(i, 8, s)
                    for k in range(4):
                        sp.dma_start(raw[:, s % 2, k, :].rearrange("p (g c) -> p g c", g=4),
                                     view[:, k, :, bass.ds(i * P, P)]).then_inc(raw_landed[s % 2], 4 * 4)
                    if s % 2 == 1:
                        m = s // 2
                        sp.wait_ge(u_lo_ready, KT)
                        sp.wait_ge(gate_free, i * 4 + (m + 1))
                        sp.dma_start(gate_in[:, :],
                                     w_mod[bass.ds(i * (2 * P) + (m // 2) * P, P),
                                           2 * D + (m % 2) * (D // 2):2 * D + (m % 2 + 1) * (D // 2)]
                                     ).then_inc(gate_landed, 16)

            for first, gate_col, proj in ((A0 // 2, GATE_A, 4), (B0 // 2, GATE_B, 6)):
                with sp.Fori(0, MERGES) as i:
                    for s in range(6):
                        w, r, c0 = (w_in, s, gate_col) if s < 4 else (w_tail, proj + s - 4, 0)
                        rows = w[r * 4 * P:(r + 1) * 4 * P, bass.ds(i * COLS + c0, COLS)]
                        wait_raw(i, 6, first + s)
                        sp.dma_start(raw[:, s % 2], rows.rearrange("(k p) c -> p k c", p=P)
                                     ).then_inc(raw_landed[s % 2], 64)
            with sp.Fori(0, D // COLS) as i:
                for s in range(4):
                    rows = w_tail[s * 4 * P:(s + 1) * 4 * P, bass.ds(i * COLS, COLS)]
                    wait_raw(i, 4, O0 // 2 + s)
                    sp.dma_start(raw[:, s % 2], rows.rearrange("(k p) c -> p k c", p=P)
                                 ).then_inc(raw_landed[s % 2], 64)
            for t in range(NT):
                sp.wait_ge(y_ready, t + 1)
                sp.dma_start(out[t * P:(t + 1) * P, :], res[:, t, :]).then_inc(stored, 16)
            sp.wait_ge(stored, 16 * NT)

        @block.scalar
        def _(act):
            def copy(dst, src):
                return act.activation(dst, src, ACT.Copy)

            def round_at(first, i, per, s):
                act.wait_ge(half_done, i * per + (first + s - LEAD + BASE))
                act.wait_ge(raw_landed[(s // 2) % 2], i * (16 * per) + 64 * (first // 4 + s // 4 + 1))
                copy(w_hi[:, s % SLOTS], raw[:, (s // 2) % 2, 2 * (s % 2):2 * (s % 2) + 2]
                     ).then_inc(hi_ready, 1)

            for events in (o_drained, pt_ready, rms_ready):
                act.sem_inc(events, BASE)
            act.wait_ge(sums_clear, 1)
            act.dma_start(mod_sum[0:1, :], b_mod[0:1, 0:2 * D]).then_inc(bias_in, 16)
            act.dma_start(gate[0:1, :], b_mod[0:1, 2 * D:3 * D]).then_inc(bias_in, 16)
            act.wait_ge(lam_sem, 1)
            act.activation(lam_exp[:, :], lam_dot[:, :], ACT.Exp).then_inc(lam_sem, 1)
            act.wait_ge(trig_ready, 1)
            act.activation(cos[:, :], cos[:, :], ACT.Sin).then_inc(sin_done, 1)
            act.wait_ge(trig_ready, 2)
            act.activation(sin[:, :], sin[:, :], ACT.Sin).then_inc(sin_done, 1)
            for k in range(KT):
                act.wait_ge(u_ready, k + 1)
                copy(act_hi[:, k, :], x_in[:, k, :]).then_inc(u_hi_ready, 1)
            for s in range(LEAD):
                act.wait_ge(raw_landed[(s // 2) % 2], 64)
                copy(w_hi[:, s], raw[:, (s // 2) % 2, 2 * (s % 2):2 * (s % 2) + 2]).then_inc(hi_ready, 1)

            with act.Fori(0, HEADS) as i:
                for s in range(HC_HALVES):
                    round_at(0, i, HC_HALVES, s + LEAD)
                    if s == 8:
                        for n, (plain, turned) in enumerate(((q_raw, q_rot), (k_raw, k_rot))):
                            act.wait_ge(bank_full[n], i * 2 + 1)
                            act.wait_ge(qk_ready, i * 2 + BASE)
                            act.wait_ge(yb_done, i + BASE)
                            act.wait_ge(ya_done, i + BASE)
                            for g in range(4):
                                to = g ^ 1
                                copy(turned[32 * to:32 * to + 32, :], acc[32 * g:32 * g + 32, n, :])
                            copy(plain[:, :], acc[:, n, :]).then_inc(bank_drained[n], 1)
                        act.wait_ge(bank_full[2], i * 2 + 1)
                        act.wait_ge(v_turned, i + BASE)
                        copy(v_f[:, :], acc[:, 2, :]).then_inc(bank_drained[2], 1)
                        act.wait_ge(half_done, i * HC_HALVES + 8 + BASE)
                        act.wait_ge(ya_done, i + BASE)
                        copy(z_a[:, :], acc[:, 3, :])
                        act.activation(e_a[:, :], acc[:, 3, :], ACT.Exp, scale=-1.0
                                       ).then_inc(bank_drained[3], 1)
                    if s == 10:
                        act.wait_ge(v_turned, i + 1 + BASE)
                        act.wait_ge(o_done, i + BASE)
                        copy(v_tok[:, :], misc[:, :]).then_inc(v_ready, 1)
                    if s in (10, 12):
                        m = (s - 10) // 2
                        act.wait_ge(max_ready, i * 2 + (m + 1))
                        act.wait_ge(p_ready if m else p_turned, i + BASE)
                        prob = prob1 if m else prob0
                        for t in (3, 2, 0, 1):
                            b, c0 = SCORE_AT[t]
                            w = (t + 1) * P
                            e = act.activation(prob[:, PROB_AT[t]:PROB_AT[t] + w], sc[:, b, c0:c0 + w],
                                               ACT.Exp, bias=neg_max[:, 4 * m + t:4 * m + t + 1],
                                               scale=DH ** -0.5,
                                               accum_out=row_sum[:, 4 * m + t:4 * m + t + 1])
                        e.then_inc(exp_done, 1)
                    if s == 14:
                        act.wait_ge(p_turned, i + 1 + BASE)
                        act.wait_ge(o_done, i + BASE)
                        copy(prob_t[:, 0:512], sc[:, 0, :])
                        copy(prob_t[:, 512:1024], sc[:, 1, :])
                        copy(prob_t[:, 1024:1280], sc[:, 2, 0:256]).then_inc(pt_ready, 1)
                    if s == 15:
                        act.wait_ge(o_done, i + 1 + BASE)
                        act.wait_ge(ya_done, i + BASE)
                        copy(o_f[:, :], misc[:, :])
                        act.activation(o_sq[:, :], misc[:, :], ACT.Square).then_inc(o_drained, 1)
                        act.wait_ge(bank_full[0], i * 2 + 2)
                        act.wait_ge(yb_done, i + BASE)
                        copy(cb_f, acc[:, 0, :]).then_inc(bank_drained[0], 1)
                        act.wait_ge(bank_full[1], i * 2 + 2)
                        copy(cc_f, acc[:, 1, :]).then_inc(bank_drained[1], 1)
                        act.wait_ge(half_done, i * HC_HALVES + 16 + BASE)
                        copy(z_b[:, :], acc[:, 3, :])
                        act.activation(e_b[:, :], acc[:, 3, :], ACT.Exp, scale=-1.0
                                       ).then_inc(bank_drained[3], 1)
                        act.wait_ge(mean_done, i + 1)
                        act.activation(rms[:, :], sc[:, 2, :], ACT.Sqrt, bias=eps_col[:, 0:1]
                                       ).then_inc(rms_ready, 1)

            with act.Fori(0, MERGES) as i:
                for s in range(MERGE_HALVES):
                    round_at(A0, i, MERGE_HALVES, s + LEAD)
                    if s == 8:
                        for n in range(4):
                            if n < 3:
                                act.wait_ge(bank_full[n], i * 2 + (A_BLOCK0 + 1))
                            else:
                                act.wait_ge(half_done, i * MERGE_HALVES + (A0 + 8 + BASE))
                            act.wait_ge(y_split, HEADS)
                            act.activation(h[:, bass.ds(i * 4 + n, 1), :].rearrange("p a t -> p (a t)"),
                                           acc[:, n, :], ACT.Sigmoid).then_inc(bank_drained[n], 1)
            with act.Fori(0, MERGES) as i:
                for s in range(MERGE_HALVES):
                    round_at(B0, i, MERGE_HALVES, s + LEAD)
                    if s == 8:
                        act.wait_ge(y_split, 2 * HEADS)
                        for n in range(4):
                            act.wait_ge(h_ready, i * 4 + BASE)
                            if n < 3:
                                act.wait_ge(bank_full[n], i * 2 + (B_BLOCK0 + 1))
                            else:
                                act.wait_ge(half_done, i * MERGE_HALVES + (B0 + 8 + BASE))
                            act.activation(sig_b[:, n, :], acc[:, n, :], ACT.Sigmoid
                                           ).then_inc(bank_drained[n], 1)
            act.wait_ge(half_done, O0 - 4 + BASE)
            for k in range(KT):
                act.wait_ge(h_ready, k + 1 + BASE)
                copy(act_hi[:, k, :], h[:, k, :]).then_inc(h_hi_ready, 1)
            act.wait_ge(half_done, O0 + BASE)
            act.wait_ge(h_ready, KT + BASE)
            act.dma_start(x_tok[:, :, :], x.rearrange("(t p) d -> p t d", p=P)).then_inc(late_in, 16)
            act.dma_start(ln_g[:, :], ln_gain.broadcast_to([P, D])).then_inc(late_in, 16)
            act.dma_start(ln_b[:, :], ln_bias.broadcast_to([P, D])).then_inc(late_in, 16)
            with act.Fori(0, D // COLS - 1) as i:
                for s in range(OUT_HALVES):
                    round_at(O0, i, OUT_HALVES, s + LEAD)
            for s in range(OUT_HALVES - LEAD):
                round_at(O0, D // COLS - 1, OUT_HALVES, s + LEAD)
            for t in range(NT):
                act.wait_ge(var_ready, t + 1)
                act.activation(rstd[:, t:t + 1], mean_var[:, t, 1:2], ACT.Sqrt, bias=eps_col[:, 0:1]
                               ).then_inc(std_ready, 1)

        @block.vector
        def _(dve):
            count = [0, 0]

            def own(ins):
                ins.then_inc(step, 1)
                count[1] += 1

            def settle(i=0, per=0):
                dve.wait_ge(step, i * per + (count[0] + count[1]))

            def close(per, times=1):
                assert per == count[1], (per, count)
                count[0] += per * times
                count[1] = 0

            def lo_half(first, i, per, s):
                dve.wait_ge(hi_ready, i * per + (first + s + 1))
                ins = dve.tensor_tensor(w_lo[:, s % SLOTS], raw[:, (s // 2) % 2, 2 * (s % 2):2 * (s % 2) + 2],
                                        w_hi[:, s % SLOTS].bitcast(F32), ALU.subtract)
                ins.then_inc(lo_ready, 1)

            for events in (qk_ready, ya_done, yb_done, p_ready, h_ready, *bank_drained):
                dve.sem_inc(events, BASE)
            dve.sem_inc(mod_free, 4)
            dve.sem_inc(lo_ready, RAW_START)
            dve.sem_inc(gate_free, 1)
            own(dve.memset(mod_sum[:, :], 0.0))
            own(dve.memset(eps_col[:, :], EPS))
            dve.wait_ge(small_in, 16 * SMALL)
            own(dve.tensor_tensor(lam_in[:, 0, :], lam_in[:, 0, :], lam_in[:, 1, :], ALU.mult))
            own(dve.tensor_tensor(lam_in[:, 2, :], lam_in[:, 2, :], lam_in[:, 3, :], ALU.mult))
            settle()
            own(dve.tensor_reduce(lam_dot[:, 0:1], lam_in[:, 0, :], AX.X, ALU.add))
            dve.tensor_reduce(lam_dot[:, 1:2], lam_in[:, 2, :], AX.X, ALU.add).then_inc(lam_sem, 1)
            ang, turns = gate[:, 0:T], gate[:, T:2 * T]
            two_pi = (6.28125, 1.9340515136718750e-03, 1.2556659146447340e-06)
            own(dve.tensor_copy(ang, sin[:, :].bitcast(I32)))
            settle()
            own(dve.tensor_scalar(ang, ang, cst[:, C_FREQ:C_FREQ + 1], None, ALU.mult))
            settle()
            magic = 1.5 * 2.0 ** 23
            for table, shift in ((cos, 0.25), (sin, 0.0)):
                own(dve.tensor_scalar(turns, ang, 1.0 / (2 * np.pi), shift, ALU.mult, ALU.add))
                settle()
                own(dve.tensor_scalar(turns, turns, magic, magic, ALU.add, ALU.subtract))
                settle()
                own(dve.scalar_tensor_tensor(table[:, :], turns, -two_pi[0], ang, ALU.mult, ALU.add))
                settle()
                for part in two_pi[1:]:
                    own(dve.scalar_tensor_tensor(table[:, :], turns, -part, table[:, :], ALU.mult, ALU.add))
                    settle()
                own(dve.tensor_scalar(table[:, :], table[:, :], shift * 2 * np.pi, 3.1415925, ALU.add, ALU.min))
                settle()
                dve.tensor_scalar(table[:, :], table[:, :], -3.1415925, None, ALU.max).then_inc(trig_ready, 1)
            dve.memset(gate[:, :], 0.0).then_inc(sums_clear, 1)
            dve.wait_ge(bias_in, 32)
            close(count[1])

            for part in range(2):
                with dve.Fori(0, KT // 4) as i:
                    for s in range(4):
                        dst = mod_sum[:, (1 - part) * D:(2 - part) * D]
                        dve.wait_ge(mod_landed[s], i * 16 + 16 * (part * 4 + 1))
                        dve.wait_ge(mod_free, i * 4 + (part * KT + s + 4))
                        dve.scalar_tensor_tensor(dst, w_mod_in[:, s, :], c_col[:, bass.ds(i * 4 + s, 1)],
                                                 dst, ALU.mult, ALU.add).then_inc(mod_free, 1)
            dve.wait_ge(mod_reduced, 1)
            own(dve.tensor_copy(mod[:, 0:KT], misc[:, 0:KT]))
            own(dve.tensor_scalar(mod[:, KT:2 * KT], misc[:, KT:2 * KT], 1.0, None, ALU.add))
            settle()
            dve.wait_ge(x_landed, 16)
            for k in range(KT):
                dve.tensor_scalar(x_in[:, k, :], x_in[:, k, :], mod[:, KT + k:KT + k + 1],
                                  mod[:, k:k + 1], ALU.mult, ALU.add).then_inc(u_ready, 1)
            for k in range(KT):
                dve.wait_ge(u_hi_ready, k + 1)
                dve.tensor_tensor(act_lo[:, k, :], x_in[:, k, :], act_hi[:, k, :].bitcast(F32), ALU.subtract
                                  ).then_inc(u_lo_ready, 1)
            dve.wait_ge(lam_sem, 2)
            own(dve.tensor_scalar(neg_lam[:, :], lam_exp[:, 1:2], -LAMBDA_INIT, None, ALU.add))
            settle()
            own(dve.tensor_tensor(neg_lam[:, :], neg_lam[:, :], lam_exp[:, 0:1], ALU.subtract))
            own(dve.tensor_scalar(gain_col[:, :], gain_col[:, :], 1.0 - LAMBDA_INIT, None, ALU.mult))
            dve.wait_ge(sin_done, 2)
            own(dve.tensor_scalar(sin[:, :], sin[:, :], cst[:, C_SIGN:C_SIGN + 1], None, ALU.mult))
            dve.wait_ge(u_lo_ready, KT)
            own(dve.memset(prod[:, 0:2], 0.0))
            settle()
            for s in range(LEAD):
                lo_half(0, 0, 0, s)
            close(count[1])

            HC_STEPS = 26

            def settle_hc():
                settle(i, HC_STEPS)

            with dve.Fori(0, HEADS) as i:
                for s in range(HC_HALVES):
                    lo_half(0, i, HC_HALVES, s + LEAD)
                    if s % 4 == 1:
                        m = s // 4
                        dst = gate[:, (m % 2) * (D // 2):(m % 2 + 1) * (D // 2)]
                        dve.wait_ge(gate_landed, i * 64 + 16 * (m + 1))
                        dve.wait_ge(gate_free, i * 4 + (m + 1))
                        dve.scalar_tensor_tensor(dst, gate_in[:, :], c_col[:, bass.ds(i * 2 + m // 2, 1)],
                                                 dst, ALU.mult, ALU.add).then_inc(gate_free, 1)
                    if s == 8:
                        dve.wait_ge(scores_done, i * 2 + BASE)
                        for n, (plain, turned, dst) in enumerate(((q_raw, q_rot, q_f), (k_raw, k_rot, k_f))):
                            dve.wait_ge(bank_drained[n], i * 2 + 1 + BASE)
                            own(dve.tensor_tensor(plain[:, :], plain[:, :], cos[:, :], ALU.mult))
                            own(dve.tensor_tensor(turned[:, :], turned[:, :], sin[:, :], ALU.mult))
                            settle_hc()
                            dve.tensor_tensor(dst[:, :], plain[:, :], turned[:, :], ALU.add).then_inc(qk_ready, 1)
                        dve.wait_ge(bank_drained[3], i * 2 + 1 + BASE)
                        own(dve.tensor_scalar(e_a[:, :], e_a[:, :], 1.0, None, ALU.add))
                        settle_hc()
                        own(dve.reciprocal(e_a[:, :], e_a[:, :]))
                        settle_hc()
                        own(dve.tensor_tensor(z_a[:, :], z_a[:, :], e_a[:, :], ALU.mult))
                    if s in (10, 12):
                        m = (s - 10) // 2
                        dve.wait_ge(scores_done, i * 2 + (m + 1 + BASE))
                        for t in range(NT):
                            b, c0 = SCORE_AT[t]
                            edge = sc[:, b, c0 + t * P:c0 + (t + 1) * P]
                            ins = dve.tensor_tensor(edge, edge, mask, ALU.min)
                        own(ins)
                        settle_hc()
                        for t in range(NT):
                            b, c0 = SCORE_AT[t]
                            ins = dve.tensor_reduce(row_max[:, t:t + 1], sc[:, b, c0:c0 + (t + 1) * P],
                                                    AX.X, ALU.max)
                        own(ins)
                        settle_hc()
                        dve.tensor_scalar(neg_max[:, 4 * m:4 * m + 4], row_max[:, :], -DH ** -0.5, None,
                                          ALU.mult).then_inc(max_ready, 1)
                    if s == 12:
                        dve.wait_ge(exp_done, i * 2 + 2)
                        own(dve.reciprocal(row_sum[:, :], row_sum[:, :]))
                        settle_hc()
                        own(dve.tensor_scalar(row_sum[:, 4:8], row_sum[:, 4:8], neg_lam[:, 0:1], None, ALU.mult))
                        settle_hc()
                        for t in range(NT):
                            a, w = PROB_AT[t], (t + 1) * P
                            own(dve.tensor_scalar(prob0[:, a:a + w], prob0[:, a:a + w], row_sum[:, t:t + 1],
                                                  None, ALU.mult))
                        for t in range(NT):
                            a, w = PROB_AT[t], (t + 1) * P
                            dve.wait_ge(step, i * HC_STEPS + (count[0] + count[1] - 3 + t))
                            ins = dve.scalar_tensor_tensor(prob0[:, a:a + w], prob1[:, a:a + w],
                                                           row_sum[:, 4 + t:5 + t], prob0[:, a:a + w],
                                                           ALU.mult, ALU.add)
                        ins.then_inc(p_ready, 1)
                    if s == 15:
                        dve.wait_ge(bank_drained[1], i * 2 + 2 + BASE)
                        dve.wait_ge(bank_full[2], i * 2 + 2)
                        dve.tensor_tensor(prod[:, 2:T + 2], acc[:, 2, :], cc_f, ALU.mult
                                          ).then_inc(bank_drained[2], 1)
                        dve.wait_ge(bank_drained[2], i * 2 + 2 + BASE)
                        own(dve.tensor_scalar(mix[:, :], prod[:, 0:T], conv_col[:, bass.ds(i * 3, 1)], None,
                                              ALU.mult))
                        settle_hc()
                        for j in (1, 2):
                            own(dve.scalar_tensor_tensor(mix[:, :], prod[:, j:j + T],
                                                         conv_col[:, bass.ds(i * 3 + j, 1)], mix[:, :],
                                                         ALU.mult, ALU.add))
                            settle_hc()
                        dve.wait_ge(bank_drained[0], i * 2 + 2 + BASE)
                        own(dve.tensor_tensor(mix[:, :], mix[:, :], cb_f, ALU.mult))
                        dve.wait_ge(bank_drained[3], i * 2 + 2 + BASE)
                        own(dve.tensor_scalar(e_b[:, :], e_b[:, :], 1.0, None, ALU.add))
                        settle_hc()
                        own(dve.reciprocal(e_b[:, :], e_b[:, :]))
                        settle_hc()
                        own(dve.tensor_tensor(z_b[:, :], z_b[:, :], e_b[:, :], ALU.mult))
                        settle_hc()
                        dve.tensor_tensor(yb[:, bass.ds(i, 1), :].rearrange("p a t -> p (a t)"),
                                          mix[:, :], z_b[:, :], ALU.mult).then_inc(yb_done, 1)
                        dve.wait_ge(rms_ready, i + 1 + BASE)
                        own(dve.reciprocal(rms[:, :], rms[:, :]))
                        settle_hc()
                        own(dve.scalar_tensor_tensor(o_f[:, :], o_f[:, :], gain_col[:, 0:1], rms[:, :],
                                                     ALU.mult, ALU.mult))
                        settle_hc()
                        dve.tensor_tensor(ya[:, bass.ds(i, 1), :].rearrange("p a t -> p (a t)"),
                                          o_f[:, :], z_a[:, :], ALU.mult).then_inc(ya_done, 1)
            close(HC_STEPS, HEADS)

            def split_y(y, done, first):
                for k in range(HEADS):
                    own(dve.tensor_copy(y_hi[:, k, :], y[:, k, :]))
                for k in range(HEADS):
                    dve.wait_ge(step, count[0] + count[1] - HEADS + 1 + k)
                    dve.tensor_tensor(y_lo[:, k, :], y[:, k, :], y_hi[:, k, :].bitcast(F32), ALU.subtract
                                      ).then_inc(y_split, 1)

            dve.wait_ge(ya_done, HEADS + BASE)
            split_y(ya, ya_done, 0)
            close(HEADS)

            with dve.Fori(0, MERGES) as i:
                for s in range(MERGE_HALVES):
                    lo_half(A0, i, MERGE_HALVES, s + LEAD)
                for n in range(4):
                    if n < 3:
                        dve.wait_ge(bank_full[n], i * 2 + (A_BLOCK0 + 2))
                    else:
                        dve.wait_ge(half_done, i * MERGE_HALVES + (A0 + MERGE_HALVES + BASE))
                    dve.wait_ge(bank_drained[n], i * 2 + (A_BLOCK0 + 1 + BASE))
                    tile = h[:, bass.ds(i * 4 + n, 1), :].rearrange("p a t -> p (a t)")
                    dve.tensor_tensor(tile, acc[:, n, :], tile, ALU.mult).then_inc(bank_drained[n], 1)
            for n in range(4):
                dve.wait_ge(gate_reduced, 1)
                own(dve.tensor_scalar(gate[:, n * 512:(n + 1) * 512], misc[:, :] if n == 3 else sc[:, n, :],
                                      float(P), None, ALU.mult))
            dve.wait_ge(half_done, B0 + BASE)
            dve.wait_ge(yb_done, HEADS + BASE)
            split_y(yb, yb_done, HEADS)
            close(4 + HEADS)

            with dve.Fori(0, MERGES) as i:
                for s in range(MERGE_HALVES):
                    lo_half(B0, i, MERGE_HALVES, s + LEAD)
                for n in range(4):
                    if n < 3:
                        dve.wait_ge(bank_full[n], i * 2 + (B_BLOCK0 + 2))
                    else:
                        dve.wait_ge(half_done, i * MERGE_HALVES + (B0 + MERGE_HALVES + BASE))
                    dve.wait_ge(bank_drained[n], i * 2 + (B_BLOCK0 + 1 + BASE))
                    dve.tensor_tensor(sig_b[:, n, :], acc[:, n, :], sig_b[:, n, :], ALU.mult
                                      ).then_inc(bank_drained[n], 1)
                for n in range(4):
                    dve.wait_ge(bank_drained[n], i * 2 + (B_BLOCK0 + 2 + BASE))
                    tile = h[:, bass.ds(i * 4 + n, 1), :].rearrange("p a t -> p (a t)")
                    dve.tensor_tensor(tile, tile, sig_b[:, n, :], ALU.add).then_inc(h_ready, 1)
            for k in range(KT):
                dve.wait_ge(h_hi_ready, k + 1)
                dve.tensor_tensor(act_lo[:, k, :], h[:, k, :], act_hi[:, k, :].bitcast(F32), ALU.subtract
                                  ).then_inc(h_split, 1)

            OUT_STEPS = 2 * NT

            def residual(i, per):
                cols = bass.ds(i * COLS, COLS)
                for t in range(NT):
                    if t < 3:
                        dve.wait_ge(bank_full[t], i + (O_BLOCK0 + 1))
                    else:
                        dve.wait_ge(half_done, i * OUT_HALVES + (O0 + OUT_HALVES + BASE))
                    dve.wait_ge(h_split, KT)
                    dve.tensor_tensor(res[:, t, cols], acc[:, t, :], gate[:, cols], ALU.mult
                                      ).then_inc(bank_drained[t], 1)
                dve.wait_ge(late_in, 48)
                for t in range(NT):
                    dve.wait_ge(bank_drained[t], i + (O_BLOCK0 + 1 + BASE))
                    own(dve.scalar_tensor_tensor(res[:, t, cols], x_tok[:, t, cols], ALPHA,
                                                 res[:, t, cols], ALU.mult, ALU.add))
                for t in range(NT):
                    dve.wait_ge(step, i * per + (count[0] + count[1] - (NT - 1)))
                    own(dve.bn_stats(stats[:, t, bass.ds(i, 1), :].rearrange("p a b -> p (a b)"),
                                     res[:, t, cols]))

            with dve.Fori(0, D // COLS - 1) as i:
                for s in range(OUT_HALVES):
                    lo_half(O0, i, OUT_HALVES, s + LEAD)
                residual(i, OUT_STEPS)
            close(OUT_STEPS, D // COLS - 1)
            last = D // COLS - 1
            for s in range(OUT_HALVES - LEAD):
                lo_half(O0, last, OUT_HALVES, s + LEAD)
            residual(last, 0)
            settle()
            for t in range(NT):
                dve.bn_aggr(mean_var[:, t, :], stats[:, t, :, :]).then_inc(var_ready, 1)
            for t in range(NT):
                dve.wait_ge(std_ready, t + 1)
                own(dve.reciprocal(rstd[:, t:t + 1], rstd[:, t:t + 1]))
                settle()
                own(dve.tensor_scalar(res[:, t, :], res[:, t, :], mean_var[:, t, 0:1], rstd[:, t:t + 1],
                                      ALU.subtract, ALU.mult))
                settle()
                own(dve.tensor_tensor(res[:, t, :], res[:, t, :], ln_g[:, :], ALU.mult))
                settle()
                dve.tensor_tensor(res[:, t, :], res[:, t, :], ln_b[:, :], ALU.add).then_inc(y_ready, 1)

        @block.tensor
        def _(pe):
            def three(dst, a_hi, a_lo, b_hi, b_lo, first, last):
                pe.matmul(dst, a_hi, b_hi, start=first, stop=False)
                pe.matmul(dst, a_hi, b_lo, start=False, stop=False)
                return pe.matmul(dst, a_lo, b_hi, start=False, stop=last)

            def half(first, i, per, s, block0, blocks, at, n_halves, m_hi, m_lo, tokens=False):
                pe.wait_ge(lo_ready, i * per + (first + s + 1 + RAW_START))
                slot = s % SLOTS
                for n in range(4):
                    if at == 0:
                        pe.wait_ge(bank_drained[n], i * blocks + block0 + BASE)
                    for kk in range(2):
                        k = 2 * at + kk
                        cols = slice(n * P, (n + 1) * P)
                        ends = at == 0 and kk == 0, at == n_halves - 1 and kk == 1
                        if tokens:
                            ins = three(acc[:, n, :], m_hi[:, k, cols], m_lo[:, k, cols],
                                        w_hi[:, slot, kk, :], w_lo[:, slot, kk, :], *ends)
                        else:
                            ins = three(acc[:, n, :], w_hi[:, slot, kk, cols], w_lo[:, slot, kk, cols],
                                        m_hi[:, k, :], m_lo[:, k, :], *ends)
                    if n == 3:
                        ins.then_inc(half_done, 1)
                    elif at == n_halves - 1:
                        ins.then_inc(bank_full[n], 1)

            for events in (v_turned, o_done, p_turned, scores_done, half_done):
                pe.sem_inc(events, BASE)
            pe.wait_ge(small_in, 16 * SMALL)
            pe.wait_ge(mod_free, 2 * KT + 4)
            for n in range(2 * KT):
                ins = pe.matmul(misc[:, n:n + 1], mod_sum[:, n * P:(n + 1) * P], one_col, start=True, stop=True)
            ins.then_inc(mod_reduced, 1)
            pe.wait_ge(u_lo_ready, KT)

            with pe.Fori(0, HEADS) as i:
                for s in range(HC_HALVES):
                    half(0, i, HC_HALVES, s, s // 8, 2, s % 8, 8, act_hi, act_lo)
                    if s == 9:
                        pe.wait_ge(bank_drained[2], i * 2 + 1 + BASE)
                        pe.wait_ge(o_drained, i + BASE)
                        for t in range(NT):
                            ins = pe.transpose(misc[:, t * P:(t + 1) * P], v_f[:, t * P:(t + 1) * P], ident)
                        ins.then_inc(v_turned, 1)
                        pe.wait_ge(pt_ready, i + BASE)
                        pe.wait_ge(rms_ready, i + BASE)
                        pe.wait_ge(qk_ready, i * 2 + 2 + BASE)
                    if s == 11:
                        pe.wait_ge(exp_done, i * 2 + 1)
                    if s in (9, 11):
                        m = (s - 9) // 2
                        rows = slice(m * DH, (m + 1) * DH)
                        for t in range(NT):
                            b, c0 = SCORE_AT[t]
                            ins = pe.matmul(sc[:, b, c0:c0 + (t + 1) * P], q_f[rows, t * P:(t + 1) * P],
                                            k_f[rows, 0:(t + 1) * P], start=True, stop=True)
                        ins.then_inc(scores_done, 1)
                    if s == 13:
                        pe.wait_ge(p_ready, i + 1 + BASE)
                        for j in range(NT):
                            b, c0 = SCORE_AT[3 - j]
                            for t in range(j, NT):
                                ins = pe.transpose(sc[:, b, c0 + (t - j) * P:c0 + (t - j + 1) * P],
                                                   prob0[:, PROB_AT[t] + j * P:PROB_AT[t] + (j + 1) * P], ident)
                        ins.then_inc(p_turned, 1)
                    if s == 14:
                        pe.wait_ge(v_ready, i + 1)
                        pe.wait_ge(pt_ready, i + 1 + BASE)
                        for j in range(NT):
                            a = PROB_AT[3 - j]
                            ins = pe.matmul(misc[:, j * P:T], v_tok[:, j * P:(j + 1) * P],
                                            prob_t[:, a:a + T - j * P], start=(j == 0), stop=(j == NT - 1))
                        ins.then_inc(o_done, 1)
                    if s == 15:
                        pe.wait_ge(o_drained, i + 1 + BASE)
                        pe.matmul(sc[:, 2, :], mean_mat, o_sq[:, :], start=True, stop=True
                                  ).then_inc(mean_done, 1)

            pe.wait_ge(gate_free, 4 * HEADS + 1)
            pe.wait_ge(rms_ready, HEADS + BASE)
            for n in range(4):
                dst = misc[:, :] if n == 3 else sc[:, n, :]
                ins = pe.matmul(dst, mean_mat, gate[:, n * 512:(n + 1) * 512], start=True, stop=True)
            ins.then_inc(gate_reduced, 1)

            for first, block0, n_split in ((A0, A_BLOCK0, HEADS), (B0, B_BLOCK0, 2 * HEADS)):
                with pe.Fori(0, MERGES) as i:
                    for s in range(8):
                        half(first, i, MERGE_HALVES, s, block0, 2, s, 8, act_hi, act_lo)
                    pe.wait_ge(y_split, n_split)
                    for s in range(8, 12):
                        half(first, i, MERGE_HALVES, s, block0 + 1, 2, s - 8, 4, y_hi, y_lo)
            with pe.Fori(0, D // COLS) as i:
                for s in range(OUT_HALVES):
                    pe.wait_ge(h_split, 2 * s + 2)
                    half(O0, i, OUT_HALVES, s, O_BLOCK0, 1, s, 8, act_hi, act_lo, tokens=True)


def kernel(x, c, positions, w_mod, b_mod, w_in, lambda_q1, lambda_k1, lambda_q2, lambda_k2,
           subln_gain, conv_w, w_proj_a, w_proj_b, w_out, ln_gain, ln_bias):
    import concourse.bacc as bacc
    from concourse.bass_utils import run_bass_kernel_spmd

    a = np.asarray
    arrays = {
        "x": a(x)[0],
        "xT": a(x)[0].T,
        "cT": a(c)[0].reshape(KT, P).T,
        "positions": a(positions),
        "w_mod": a(w_mod)[0],
        "b_mod": a(b_mod),
        "w_in": a(w_in)[0],
        "lams": np.concatenate([a(v) for v in (lambda_q1, lambda_k1, lambda_q2, lambda_k2)], axis=1),
        "gain": a(subln_gain).T,
        "conv_w": a(conv_w)[0].reshape(3, HEADS, P).transpose(2, 1, 0).reshape(P, 3 * HEADS),
        "w_tail": np.concatenate([a(w_out)[0], a(w_proj_a)[0], a(w_proj_b)[0]]),
        "ln_gain": a(ln_gain),
        "ln_bias": a(ln_bias),
        "consts": constants(),
    }
    nc = bacc.Bacc("TRN2", target_bir_lowering=False, num_devices=1)
    ins, sent = {}, {}
    for name, v in arrays.items():
        v = np.ascontiguousarray(v)
        sent[f"in_{name}"] = v
        ins[name] = nc.dram_tensor(f"in_{name}", v.shape, mybir.dt.from_np(v.dtype), kind="ExternalInput").ap()
    out = nc.dram_tensor("out", (T, D), F32, kind="ExternalOutput").ap()
    decoder_block(nc, out=out, **ins)
    r = run_bass_kernel_spmd(nc, [sent], core_ids=[0])
    return r.results[0]["out"].reshape(1, T, D)
```

```python
from contextlib import ExitStack

import numpy as np

import concourse.bass as bass
from concourse import mybir

F32 = mybir.dt.float32
F32R = mybir.dt.float32r
I32 = mybir.dt.int32
ALU = mybir.AluOpType
ACT = mybir.ActivationFunctionType
AX = mybir.AxisListType

P = 128
D = 2048
T = 512
KT = D // P
HEADS = 8
DH = 64
SEG = 1024
NT = T // P
COLS = 512
GATE_A, GATE_B = 8 * SEG, 8 * SEG + D
EPS = 1e-5
ALPHA = 2.0 ** 0.25
LAMBDA_INIT = 0.8 - 0.6
BIG = 3.0e38
RAW_START = 4
BASE = 1
GROUPS = 4
MOD_UNITS = 8
MOD_SLOTS = 4
MOD_STEPS = 4
LEAD = 3
SLOTS = 4

HC_HALVES, HC_BLOCKS = 16, 2
MERGE_HALVES, MERGE_BLOCKS = 12, 2
OUT_HALVES, OUT_BLOCKS = 8, 1
MERGES = D // COLS
HEAD0 = HC_HALVES // 2
A0, A_BLOCK0 = HEADS * HC_HALVES, HEADS * HC_BLOCKS
B0, B_BLOCK0 = A0 + MERGES * MERGE_HALVES, A_BLOCK0 + MERGES * MERGE_BLOCKS
O0, O_BLOCK0 = B0 + MERGES * MERGE_HALVES, B_BLOCK0 + MERGES * MERGE_BLOCKS
HALVES = O0 + (D // COLS) * OUT_HALVES

SCORE_AT = {3: (0, 0), 2: (1, 0), 0: (1, 384), 1: (2, 0)}
PROB_AT = {3: 0, 2: 512, 0: 896, 1: 1024}
PACKED = 1280

C_IDENT, C_MASK, C_MEAN, C_FREQ, C_SIGN, C_ONE, C_WIDTH = 0, 128, 256, 384, 385, 386, 387


def constants():
    c = np.zeros((P, C_WIDTH), np.float32)
    c[:, C_IDENT:C_IDENT + P] = np.eye(P)
    q, k = np.meshgrid(np.arange(P), np.arange(P), indexing="ij")
    c[:, C_MASK:C_MASK + P] = np.where(k <= q, BIG, -BIG)
    c[:, C_MEAN:C_MEAN + P] = 1.0 / P
    freq = (10000.0 ** (-np.arange(0, DH, 2) / DH)).astype(np.float32)
    c[:, C_FREQ] = np.tile(freq, 4)
    c[:, C_SIGN] = np.where((np.arange(P) // 32) % 2 == 0, -1.0, 1.0)
    c[:, C_ONE] = 1.0
    return c


def decoder_block(nc, x, xT, cT, positions, w_mod, b_mod, b_cols, w_in, lams, gain, conv_w, w_tail,
                  ln_gain, ln_bias, consts, out):
    ctx = ExitStack()
    with ctx:
        def sb(name, shape, dt=F32, scope=None):
            return (scope or ctx).enter_context(nc.sbuf_tensor(name, shape, dt))

        def sem(name):
            return ctx.enter_context(nc.semaphore(name))

        raw = sb("raw", [P, 2, 4, COLS])
        w_hi = sb("w_hi", [P, SLOTS, 2, COLS], F32R)
        w_lo = sb("w_lo", [P, SLOTS, 2, COLS], F32R)
        act_hi = sb("act_hi", [P, KT, T], F32R)
        act_lo = sb("act_lo", [P, KT, T], F32R)
        gate = sb("gate", [P, D])
        cst = sb("cst", [P, C_WIDTH])
        cos = sb("cos", [P, T])
        sin = sb("sin", [P, T])
        c_col = sb("c_col", [P, KT])
        b_col = sb("b_col", [P, 2 * KT])
        conv_col = sb("conv_col", [P, HEADS * 3])
        gain_col = sb("gain_col", [P, 1])
        eps_col = sb("eps_col", [P, 1])
        mod = sb("mod", [P, 2 * KT])
        lam_in = sb("lam_in", [P, 4, DH])
        lam_dot = sb("lam_dot", [P, 2])
        lam_exp = sb("lam_exp", [P, 2])
        neg_lam = sb("neg_lam", [P, 1])
        row_max = sb("row_max", [P, 4])
        neg_max = sb("neg_max", [P, 8])
        row_sum = sb("row_sum", [P, 8])
        stats = sb("stats", [P, NT, D // COLS, 6])
        mean_var = sb("mean_var", [P, NT, 2])
        rstd = sb("rstd", [P, NT])

        def stage(name_shapes):
            scope = ExitStack()
            made = [sb(n, s, d, scope) for n, s, d in name_shapes]
            scope.close()
            return made

        with ExitStack() as place:
            mod_sum = sb("mod_sum", [P, 2, 2, COLS], F32, place)
            place.close()
        with ExitStack() as place:
            sig_b = sb("sig_b", [P, 4, T], F32, place)
            place.close()
        ln_g, ln_b = stage([("ln_g", [P, D], F32), ("ln_b", [P, D], F32)])
        yb = sb("yb", [P, HEADS, T])
        x_in, w_mod_in = stage([("x_in", [P, KT, T], F32),
                                ("w_mod_in", [P, MOD_SLOTS, 2, 2, COLS], F32)])
        (ya, gate_in, q_raw, q_rot, k_raw, k_rot, q_f, k_f, v_f, v_tok, z_a, e_a, prob0, prob1,
         prob_t, o_f, prod, mix) = stage([
            ("ya", [P, HEADS, T], F32), ("gate_in", [P, D // 2], F32),
            ("q_raw", [P, T], F32), ("q_rot", [P, T], F32), ("k_raw", [P, T], F32),
            ("k_rot", [P, T], F32), ("q_f", [P, T], F32), ("k_f", [P, T], F32),
            ("v_f", [P, T], F32), ("v_tok", [P, T], F32), ("z_a", [P, T], F32),
            ("e_a", [P, T], F32), ("prob0", [P, PACKED], F32), ("prob1", [P, PACKED], F32),
            ("prob_t", [P, PACKED], F32), ("o_f", [P, T], F32), ("prod", [P, T + 2], F32),
            ("mix", [P, T], F32)])
        cb_f, cc_f = prob1[:, 0:T], prob1[:, T:2 * T]
        z_b, e_b, o_sq, rms = q_raw, q_rot, k_raw, k_rot
        h, y_hi, y_lo = stage([("h", [P, KT, T], F32), ("y_hi", [P, HEADS, T], F32R),
                               ("y_lo", [P, HEADS, T], F32R)])
        res, x_tok = stage([("res", [P, NT, D], F32), ("x_tok", [P, NT, D], F32)])

        acc = ctx.enter_context(nc.psum_tensor("acc", [P, 4, COLS], F32))
        sc = ctx.enter_context(nc.psum_tensor("sc", [P, 3, 512], F32))
        misc = ctx.enter_context(nc.psum_tensor("misc", [P, 512], F32))

        ident = cst[:, C_IDENT:C_IDENT + P]
        mask = cst[:, C_MASK:C_MASK + P]
        mean_mat = cst[:, C_MEAN:C_MEAN + P]
        one_col = cst[:, C_ONE:C_ONE + 1]

        small_in = sem("small_in")
        x_landed = sem("x_landed")
        bias_in = sem("bias_in")
        sums_clear = sem("sums_clear")
        mod_landed = [sem(f"mod_landed{s}") for s in range(4)]
        mod_step = sem("mod_step")
        sum_clear = sem("sum_clear")
        mod_reduced = sem("mod_reduced")
        mod_ready = sem("mod_ready")
        lam_sem = sem("lam_sem")
        trig_ready = sem("trig_ready")
        sin_done = sem("sin_done")
        u_ready = sem("u_ready")
        u_lo_ready = sem("u_lo_ready")
        raw_landed = [sem("raw_landed0"), sem("raw_landed1")]
        hi_ready = sem("hi_ready")
        lo_ready = sem("lo_ready")
        half_done = sem("half_done")
        bank_full = [sem(f"bank_full{n}") for n in range(3)]
        bank_drained = [sem(f"bank_drained{n}") for n in range(4)]
        gate_landed = sem("gate_landed")
        gate_free = sem("gate_free")
        gate_reduced = sem("gate_reduced")
        gate_ready = sem("gate_ready")
        qk_swapped = sem("qk_swapped")
        qk_ready = sem("qk_ready")
        v_turned = sem("v_turned")
        v_ready = sem("v_ready")
        scores_done = sem("scores_done")
        max_ready = sem("max_ready")
        exp_done = sem("exp_done")
        p_ready = sem("p_ready")
        p_turned = sem("p_turned")
        pt_ready = sem("pt_ready")
        o_done = sem("o_done")
        o_drained = sem("o_drained")
        mean_done = sem("mean_done")
        rms_ready = sem("rms_ready")
        ya_done = sem("ya_done")
        yb_done = sem("yb_done")
        y_split = sem("y_split")
        h_ready = sem("h_ready")
        h_hi_ready = sem("h_hi_ready")
        h_split = sem("h_split")
        late_in = sem("late_in")
        step = sem("step")
        var_ready = sem("var_ready")
        std_ready = sem("std_ready")
        y_ready = sem("y_ready")
        stored = sem("stored")

        SMALL = 7
        block = ctx.enter_context(nc.Block())

        @block.gpsimd
        def _(pool):
            for g in range(GROUPS):
                if g >= 2:
                    pool.wait_ge(mod_reduced, g - 1)
                pool.memset(mod_sum[:, g % 2], 0.0).then_inc(sum_clear, 1)
            pool.wait_ge(u_lo_ready, KT)
            with pool.Fori(0, HEADS) as i:
                for m in range(4):
                    pool.wait_ge(gate_free, i * 4 + (m + 1))
                    pool.dma_start(gate_in[:, :],
                                   w_mod[bass.ds(i * (2 * P) + (m // 2) * P, P),
                                         2 * D + (m % 2) * (D // 2):2 * D + (m % 2 + 1) * (D // 2)]
                                   ).then_inc(gate_landed, 16)

        @block.sync
        def _(sp):
            sp.dma_start(c_col[:, :], cT).then_inc(small_in, 16)
            sp.dma_start(cst[:, :], consts).then_inc(small_in, 16)
            sp.dma_start(sin[:, :].bitcast(I32), positions.broadcast_to([P, T])).then_inc(small_in, 16)
            sp.dma_start(conv_col[:, :], conv_w).then_inc(small_in, 16)
            sp.dma_start(b_col[:, :], b_cols).then_inc(small_in, 16)
            sp.dma_start(gain_col[:, :], gain).then_inc(small_in, 16)
            sp.dma_start(lam_in[:, :, :].rearrange("p a d -> p (a d)"),
                         lams.broadcast_to([P, 4 * DH])).then_inc(small_in, 16)
            def head_unit(s, col, raw_slot):
                rows = w_in[s * 4 * P:(s + 1) * 4 * P, 0:4 * SEG]
                quarter(rows, col, raw_slot)

            def conv_unit(s, col, raw_slot):
                rows = w_in[s * 4 * P:(s + 1) * 4 * P, 4 * SEG:8 * SEG]
                quarter(rows, col, raw_slot)

            def quarter(rows, col, raw_slot):
                view = rows.rearrange("(k p) (g c) -> p k g c", p=P, g=4)
                for k in range(4):
                    sp.dma_start(raw[:, raw_slot, k, :].rearrange("p (g c) -> p g c", g=4),
                                 view[:, k, :, bass.ds(col, P)]).then_inc(raw_landed[raw_slot], 16)

            for g in range(GROUPS):
                for n in range(MOD_UNITS):
                    unit = g * MOD_UNITS + n
                    if unit >= MOD_SLOTS:
                        sp.wait_ge(mod_step, (unit + 1) * MOD_STEPS)
                    for part, first_col in enumerate((D, 0)):
                        cols = slice(first_col + g * COLS, first_col + (g + 1) * COLS)
                        rows = w_mod[n * 2 * P:(n + 1) * 2 * P, cols]
                        sp.dma_start(w_mod_in[:, unit % MOD_SLOTS, part],
                                     rows.rearrange("(k p) c -> p k c", p=P)
                                     ).then_inc(mod_landed[unit % MOD_SLOTS], 16)
                    if n == 3:
                        sp.dma_start(x_in[:, 4 * g:4 * g + 4, :],
                                     xT[g * 4 * P:(g + 1) * 4 * P, :].rearrange("(k p) t -> p k t", p=P)
                                     ).then_inc(x_landed, 16)
                    if n == 5:
                        if g >= 2:
                            sp.wait_ge(lo_ready, 2 * (g - 1) + RAW_START)
                        head_unit(g, 0, g % 2)

            def wait_raw(i, per, u):
                sp.wait_ge(lo_ready, i * (2 * per) + (2 * (u - 1) + RAW_START))

            with sp.Fori(0, HEADS - 1) as i:
                for s in range(8):
                    wait_raw(i, 8, 4 + s)
                    if s < 4:
                        conv_unit(s, i * P, s % 2)
                    else:
                        head_unit(s - 4, i * P + P, s % 2)
            for s in range(4):
                wait_raw(HEADS - 1, 8, 4 + s)
                conv_unit(s, (HEADS - 1) * P, s % 2)

            for first, gate_col, proj in ((A0 // 2, GATE_A, 4), (B0 // 2, GATE_B, 6)):
                with sp.Fori(0, MERGES) as i:
                    for s in range(6):
                        w, r, c0 = (w_in, s, gate_col) if s < 4 else (w_tail, proj + s - 4, 0)
                        rows = w[r * 4 * P:(r + 1) * 4 * P, bass.ds(i * COLS + c0, COLS)]
                        wait_raw(i, 6, first + s)
                        sp.dma_start(raw[:, s % 2], rows.rearrange("(k p) c -> p k c", p=P)
                                     ).then_inc(raw_landed[s % 2], 64)
            with sp.Fori(0, D // COLS) as i:
                for s in range(4):
                    rows = w_tail[s * 4 * P:(s + 1) * 4 * P, bass.ds(i * COLS, COLS)]
                    wait_raw(i, 4, O0 // 2 + s)
                    sp.dma_start(raw[:, s % 2], rows.rearrange("(k p) c -> p k c", p=P)
                                 ).then_inc(raw_landed[s % 2], 64)
            for n in range(2 * NT):
                t, cols = n // 2, slice((n % 2) * (D // 2), (n % 2 + 1) * (D // 2))
                sp.wait_ge(y_ready, n + 1)
                sp.dma_start(out[t * P:(t + 1) * P, cols], res[:, t, cols]).then_inc(stored, 16)
            sp.wait_ge(stored, 16 * 2 * NT)

        @block.scalar
        def _(act):
            def copy(dst, src):
                return act.activation(dst, src, ACT.Copy)

            def round_at(first, i, per, s):
                act.wait_ge(half_done, i * per + (first + s - LEAD + BASE))
                act.wait_ge(raw_landed[(s // 2) % 2], i * (16 * per) + 64 * (first // 4 + s // 4 + 1))
                copy(w_hi[:, s % SLOTS], raw[:, (s // 2) % 2, 2 * (s % 2):2 * (s % 2) + 2]
                     ).then_inc(hi_ready, 1)

            for events in (o_drained, pt_ready, rms_ready):
                act.sem_inc(events, BASE)
            def round_first(f):
                if f >= SLOTS:
                    act.wait_ge(half_done, f - LEAD + BASE)
                act.wait_ge(raw_landed[(f // 2) % 2], 64 * (f // 4 + 1))
                copy(w_hi[:, f % SLOTS], raw[:, (f // 2) % 2, 2 * (f % 2):2 * (f % 2) + 2]
                     ).then_inc(hi_ready, 1)

            for g in range(GROUPS):
                if g == 0:
                    round_first(0)
                    round_first(1)
                act.wait_ge(mod_ready, g + 1)
                act.wait_ge(x_landed, 16 * (g + 1))
                for k in range(4 * g, 4 * g + 4):
                    args = dict(scale=mod[:, KT + k:KT + k + 1], bias=mod[:, k:k + 1])
                    act.activation(act_hi[:, k, :], x_in[:, k, :], ACT.Identity, **args)
                    act.activation(x_in[:, k, :], x_in[:, k, :], ACT.Identity, **args).then_inc(u_ready, 1)
                if g + 1 < GROUPS:
                    round_first(2 * g + 2)
                    round_first(2 * g + 3)
            for f in range(2 * GROUPS, 2 * GROUPS + LEAD - 1):
                round_first(f)
            act.wait_ge(lam_sem, 1)
            act.activation(lam_exp[:, :], lam_dot[:, :], ACT.Exp).then_inc(lam_sem, 1)
            act.wait_ge(trig_ready, 1)
            act.activation(cos[:, :], cos[:, :], ACT.Sin).then_inc(sin_done, 1)
            act.wait_ge(trig_ready, 2)
            act.activation(sin[:, :], sin[:, :], ACT.Sin).then_inc(sin_done, 1)
            round_first(2 * GROUPS + LEAD - 1)
            act.wait_ge(sums_clear, 1)
            act.dma_start(gate[0:1, :], b_mod[0:1, 2 * D:3 * D]).then_inc(bias_in, 16)

            def drain_head(i):
                for n, (plain, turned) in enumerate(((q_raw, q_rot), (k_raw, k_rot))):
                    act.wait_ge(bank_full[n], i * 2 + 1)
                    act.wait_ge(qk_ready, i * 2 + BASE)
                    act.wait_ge(yb_done, i + BASE)
                    act.wait_ge(ya_done, i + BASE)
                    copy(plain[:, :], acc[:, n, :]).then_inc(bank_drained[n], 1)
                act.wait_ge(bank_full[2], i * 2 + 1)
                act.wait_ge(v_turned, i + BASE)
                copy(v_f[:, :], acc[:, 2, :]).then_inc(bank_drained[2], 1)
                for n, (plain, turned) in enumerate(((q_raw, q_rot), (k_raw, k_rot))):
                    act.wait_ge(bank_drained[n], i * 2 + 1 + BASE)
                    for g in range(4):
                        to = g ^ 1
                        ins = copy(turned[32 * to:32 * to + 32, :], plain[32 * g:32 * g + 32, :])
                    ins.then_inc(qk_swapped, 1)
                act.wait_ge(half_done, i * HC_HALVES + HEAD0 + BASE)
                copy(z_a[:, :], acc[:, 3, :])
                act.activation(e_a[:, :], acc[:, 3, :], ACT.Exp, scale=-1.0
                               ).then_inc(bank_drained[3], 1)

            def attend_and_convolve(i, s):
                if s == 2:
                    act.wait_ge(v_turned, i + 1 + BASE)
                    act.wait_ge(o_done, i + BASE)
                    copy(v_tok[:, :], misc[:, :]).then_inc(v_ready, 1)
                if s in (2, 4):
                    m = (s - 2) // 2
                    act.wait_ge(max_ready, i * 2 + (m + 1))
                    act.wait_ge(p_ready if m else p_turned, i + BASE)
                    prob = prob1 if m else prob0
                    for t in (3, 2, 0, 1):
                        b, c0 = SCORE_AT[t]
                        w = (t + 1) * P
                        e = act.activation(prob[:, PROB_AT[t]:PROB_AT[t] + w], sc[:, b, c0:c0 + w],
                                           ACT.Exp, bias=neg_max[:, 4 * m + t:4 * m + t + 1],
                                           scale=DH ** -0.5,
                                           accum_out=row_sum[:, 4 * m + t:4 * m + t + 1])
                    e.then_inc(exp_done, 1)
                if s == 6:
                    act.wait_ge(p_turned, i + 1 + BASE)
                    act.wait_ge(o_done, i + BASE)
                    copy(prob_t[:, 0:512], sc[:, 0, :])
                    copy(prob_t[:, 512:1024], sc[:, 1, :])
                    copy(prob_t[:, 1024:1280], sc[:, 2, 0:256]).then_inc(pt_ready, 1)
                if s == 7:
                    act.wait_ge(o_done, i + 1 + BASE)
                    act.wait_ge(ya_done, i + BASE)
                    copy(o_f[:, :], misc[:, :])
                    act.activation(o_sq[:, :], misc[:, :], ACT.Square).then_inc(o_drained, 1)
                    act.wait_ge(bank_full[0], i * 2 + 2)
                    act.wait_ge(yb_done, i + BASE)
                    copy(cb_f, acc[:, 0, :]).then_inc(bank_drained[0], 1)
                    act.wait_ge(bank_full[1], i * 2 + 2)
                    copy(cc_f, acc[:, 1, :]).then_inc(bank_drained[1], 1)
                    act.wait_ge(half_done, i * HC_HALVES + HC_HALVES + BASE)
                    copy(z_b[:, :], acc[:, 3, :])
                    act.activation(e_b[:, :], acc[:, 3, :], ACT.Exp, scale=-1.0
                                   ).then_inc(bank_drained[3], 1)
                    act.wait_ge(mean_done, i + 1)
                    act.activation(rms[:, :], sc[:, 2, :], ACT.Sqrt, bias=eps_col[:, 0:1]
                                   ).then_inc(rms_ready, 1)

            drain_head(0)
            with act.Fori(0, HEADS - 1) as i:
                for s in range(HC_HALVES):
                    round_at(HEAD0, i, HC_HALVES, s + LEAD)
                    if s < 8:
                        attend_and_convolve(i, s)
                drain_head(i + 1)
            for s in range(8):
                round_at(HEAD0, HEADS - 1, HC_HALVES, s + LEAD)
                attend_and_convolve(HEADS - 1, s)

            with act.Fori(0, MERGES) as i:
                for s in range(MERGE_HALVES):
                    round_at(A0, i, MERGE_HALVES, s + LEAD)
                    if s == 7:
                        for n in range(4):
                            if n < 3:
                                act.wait_ge(bank_full[n], i * 2 + (A_BLOCK0 + 1))
                            else:
                                act.wait_ge(half_done, i * MERGE_HALVES + (A0 + 8 + BASE))
                            act.wait_ge(y_split, HEADS)
                            act.activation(h[:, bass.ds(i * 4 + n, 1), :].rearrange("p a t -> p (a t)"),
                                           acc[:, n, :], ACT.Sigmoid).then_inc(bank_drained[n], 1)
            def merge_b(i, last=False):
                for s in range(MERGE_HALVES):
                    round_at(B0, i, MERGE_HALVES, s + LEAD)
                    if s == 7:
                        act.wait_ge(y_split, 2 * HEADS)
                        for n in range(4):
                            act.wait_ge(h_ready, i * 4 + BASE)
                            if n < 3:
                                act.wait_ge(bank_full[n], i * 2 + (B_BLOCK0 + 1))
                            else:
                                act.wait_ge(half_done, i * MERGE_HALVES + (B0 + 8 + BASE))
                            act.activation(sig_b[:, n, :], acc[:, n, :], ACT.Sigmoid
                                           ).then_inc(bank_drained[n], 1)
                    if last and s > 7:
                        act.wait_ge(half_done, O0 - 4 + BASE)
                        for k in range(3 * (s - 8), 3 * (s - 8) + 3):
                            copy(act_hi[:, k, :], h[:, k, :]).then_inc(h_hi_ready, 1)

            with act.Fori(0, MERGES - 1) as i:
                merge_b(i)
            merge_b(MERGES - 1, last=True)
            for k in range(KT - 4, KT):
                act.wait_ge(h_ready, k + 1 + BASE)
                copy(act_hi[:, k, :], h[:, k, :]).then_inc(h_hi_ready, 1)
            act.wait_ge(half_done, O0 + BASE)
            act.wait_ge(h_ready, KT + BASE)
            act.dma_start(x_tok[:, :, :], x.rearrange("(t p) d -> p t d", p=P)).then_inc(late_in, 16)
            act.dma_start(ln_g[:, :], ln_gain.broadcast_to([P, D])).then_inc(late_in, 16)
            act.dma_start(ln_b[:, :], ln_bias.broadcast_to([P, D])).then_inc(late_in, 16)
            with act.Fori(0, D // COLS - 1) as i:
                for s in range(OUT_HALVES):
                    round_at(O0, i, OUT_HALVES, s + LEAD)
            for s in range(OUT_HALVES - LEAD):
                round_at(O0, D // COLS - 1, OUT_HALVES, s + LEAD)
            for t in range(NT):
                act.wait_ge(var_ready, t + 1)
                act.activation(rstd[:, t:t + 1], mean_var[:, t, 1:2], ACT.Sqrt, bias=eps_col[:, 0:1]
                               ).then_inc(std_ready, 1)

        @block.vector
        def _(dve):
            count = [0, 0]

            def own(ins):
                ins.then_inc(step, 1)
                count[1] += 1

            def settle(i=0, per=0):
                dve.wait_ge(step, i * per + (count[0] + count[1]))

            def close(per, times=1):
                assert per == count[1], (per, count)
                count[0] += per * times
                count[1] = 0

            def lo_half(first, i, per, s):
                dve.wait_ge(hi_ready, i * per + (first + s + 1))
                ins = dve.tensor_tensor(w_lo[:, s % SLOTS], raw[:, (s // 2) % 2, 2 * (s % 2):2 * (s % 2) + 2],
                                        w_hi[:, s % SLOTS].bitcast(F32), ALU.subtract)
                ins.then_inc(lo_ready, 1)

            for events in (qk_ready, ya_done, yb_done, p_ready, h_ready, *bank_drained):
                dve.sem_inc(events, BASE)
            dve.sem_inc(lo_ready, RAW_START)
            dve.sem_inc(mod_step, MOD_SLOTS * MOD_STEPS)
            dve.sem_inc(gate_free, 1)
            own(dve.memset(eps_col[:, :], EPS))
            dve.wait_ge(small_in, 16 * SMALL)

            def sum_unit(unit):
                g, n = divmod(unit, MOD_UNITS)
                dve.wait_ge(mod_landed[unit % MOD_SLOTS], 32 * (unit // MOD_SLOTS + 1))
                for a in range(2):
                    for part in range(2):
                        e = MOD_STEPS * unit + 2 * a + part
                        dst = mod_sum[:, g % 2, part, :]
                        if e % (MOD_UNITS * MOD_STEPS) >= 2:
                            dve.wait_ge(mod_step, e - 1 + MOD_SLOTS * MOD_STEPS)
                        else:
                            dve.wait_ge(sum_clear, g + 1)
                        dve.scalar_tensor_tensor(dst, w_mod_in[:, unit % MOD_SLOTS, part, a, :],
                                                 c_col[:, 2 * n + a:2 * n + a + 1], dst,
                                                 ALU.mult, ALU.add).then_inc(mod_step, 1)

            def columns(g):
                dve.wait_ge(mod_reduced, g + 1)
                four = slice(4 * g, 4 * g + 4)
                own(dve.tensor_tensor(mod[:, four], misc[:, 8 * g + 4:8 * g + 8], b_col[:, four], ALU.add))
                dve.scalar_tensor_tensor(mod[:, KT + 4 * g:KT + 4 * g + 4], misc[:, 8 * g:8 * g + 4], 1.0,
                                         b_col[:, KT + 4 * g:KT + 4 * g + 4], ALU.add, ALU.add
                                         ).then_inc(mod_ready, 1)

            def u_lo(g):
                for k in range(4 * g, 4 * g + 4):
                    dve.wait_ge(u_ready, k + 1)
                    dve.tensor_tensor(act_lo[:, k, :], x_in[:, k, :], act_hi[:, k, :].bitcast(F32),
                                      ALU.subtract).then_inc(u_lo_ready, 1)

            for g in range(GROUPS):
                for n in range(MOD_UNITS):
                    sum_unit(g * MOD_UNITS + n)
                    if g and n == 0:
                        columns(g - 1)
                    if g and n == 3:
                        u_lo(g - 1)
                lo_half(0, 0, 0, 2 * g)
                lo_half(0, 0, 0, 2 * g + 1)
            columns(GROUPS - 1)
            u_lo(GROUPS - 1)
            for f in range(2 * GROUPS, 2 * GROUPS + LEAD - 1):
                lo_half(0, 0, 0, f)
            own(dve.tensor_tensor(lam_in[:, 0, :], lam_in[:, 0, :], lam_in[:, 1, :], ALU.mult))
            own(dve.tensor_tensor(lam_in[:, 2, :], lam_in[:, 2, :], lam_in[:, 3, :], ALU.mult))
            settle()
            own(dve.tensor_reduce(lam_dot[:, 0:1], lam_in[:, 0, :], AX.X, ALU.add))
            dve.tensor_reduce(lam_dot[:, 1:2], lam_in[:, 2, :], AX.X, ALU.add).then_inc(lam_sem, 1)
            ang, turns = gate[:, 0:T], gate[:, T:2 * T]
            two_pi = (6.28125, 1.9340515136718750e-03, 1.2556659146447340e-06)
            own(dve.tensor_copy(ang, sin[:, :].bitcast(I32)))
            settle()
            own(dve.tensor_scalar(ang, ang, cst[:, C_FREQ:C_FREQ + 1], None, ALU.mult))
            settle()
            magic = 1.5 * 2.0 ** 23
            for table, shift in ((cos, 0.25), (sin, 0.0)):
                own(dve.tensor_scalar(turns, ang, 1.0 / (2 * np.pi), shift, ALU.mult, ALU.add))
                settle()
                own(dve.tensor_scalar(turns, turns, magic, magic, ALU.add, ALU.subtract))
                settle()
                own(dve.scalar_tensor_tensor(table[:, :], turns, -two_pi[0], ang, ALU.mult, ALU.add))
                settle()
                for part in two_pi[1:]:
                    own(dve.scalar_tensor_tensor(table[:, :], turns, -part, table[:, :], ALU.mult, ALU.add))
                    settle()
                own(dve.tensor_scalar(table[:, :], table[:, :], shift * 2 * np.pi, 3.1415925, ALU.add, ALU.min))
                settle()
                dve.tensor_scalar(table[:, :], table[:, :], -3.1415925, None, ALU.max).then_inc(trig_ready, 1)
            dve.memset(gate[:, :], 0.0).then_inc(sums_clear, 1)
            lo_half(0, 0, 0, 2 * GROUPS + LEAD - 1)
            dve.wait_ge(lam_sem, 2)
            own(dve.tensor_scalar(neg_lam[:, :], lam_exp[:, 1:2], -LAMBDA_INIT, None, ALU.add))
            settle()
            own(dve.tensor_tensor(neg_lam[:, :], neg_lam[:, :], lam_exp[:, 0:1], ALU.subtract))
            own(dve.tensor_scalar(gain_col[:, :], gain_col[:, :], 1.0 - LAMBDA_INIT, None, ALU.mult))
            dve.wait_ge(sin_done, 2)
            own(dve.tensor_scalar(sin[:, :], sin[:, :], cst[:, C_SIGN:C_SIGN + 1], None, ALU.mult))
            dve.wait_ge(u_lo_ready, KT)
            own(dve.memset(prod[:, 0:2], 0.0))
            settle()

            HC_STEPS = 26

            def rotate(i, settle_hc):
                dve.wait_ge(scores_done, i * 2 + BASE)
                for n, (plain, turned, dst) in enumerate(((q_raw, q_rot, q_f), (k_raw, k_rot, k_f))):
                    dve.wait_ge(qk_swapped, i * 2 + n + 1)
                    own(dve.tensor_tensor(plain[:, :], plain[:, :], cos[:, :], ALU.mult))
                    own(dve.tensor_tensor(turned[:, :], turned[:, :], sin[:, :], ALU.mult))
                    settle_hc()
                    dve.tensor_tensor(dst[:, :], plain[:, :], turned[:, :], ALU.add).then_inc(qk_ready, 1)
                dve.wait_ge(bank_drained[3], i * 2 + 1 + BASE)
                own(dve.tensor_scalar(e_a[:, :], e_a[:, :], 1.0, None, ALU.add))
                settle_hc()
                own(dve.reciprocal(e_a[:, :], e_a[:, :]))
                settle_hc()
                own(dve.tensor_tensor(z_a[:, :], z_a[:, :], e_a[:, :], ALU.mult))

            def attend_and_convolve(i, s, settle_hc, base):
                if s % 2 == 1:
                    m = s // 2
                    dst = gate[:, (m % 2) * (D // 2):(m % 2 + 1) * (D // 2)]
                    dve.wait_ge(gate_landed, i * 64 + 16 * (m + 1))
                    dve.wait_ge(gate_free, i * 4 + (m + 1))
                    dve.scalar_tensor_tensor(dst, gate_in[:, :], c_col[:, bass.ds(i * 2 + m // 2, 1)],
                                             dst, ALU.mult, ALU.add).then_inc(gate_free, 1)
                if s in (2, 4):
                    m = (s - 2) // 2
                    dve.wait_ge(scores_done, i * 2 + (m + 1 + BASE))
                    for t in range(NT):
                        b, c0 = SCORE_AT[t]
                        edge = sc[:, b, c0 + t * P:c0 + (t + 1) * P]
                        ins = dve.tensor_tensor(edge, edge, mask, ALU.min)
                    own(ins)
                    settle_hc()
                    for t in range(NT):
                        b, c0 = SCORE_AT[t]
                        ins = dve.tensor_reduce(row_max[:, t:t + 1], sc[:, b, c0:c0 + (t + 1) * P],
                                                AX.X, ALU.max)
                    own(ins)
                    settle_hc()
                    dve.tensor_scalar(neg_max[:, 4 * m:4 * m + 4], row_max[:, :], -DH ** -0.5, None,
                                      ALU.mult).then_inc(max_ready, 1)
                if s == 4:
                    dve.wait_ge(exp_done, i * 2 + 2)
                    own(dve.reciprocal(row_sum[:, :], row_sum[:, :]))
                    settle_hc()
                    own(dve.tensor_scalar(row_sum[:, 4:8], row_sum[:, 4:8], neg_lam[:, 0:1], None, ALU.mult))
                    settle_hc()
                    for t in range(NT):
                        a, w = PROB_AT[t], (t + 1) * P
                        own(dve.tensor_scalar(prob0[:, a:a + w], prob0[:, a:a + w], row_sum[:, t:t + 1],
                                              None, ALU.mult))
                    for t in range(NT):
                        a, w = PROB_AT[t], (t + 1) * P
                        dve.wait_ge(step, base + (count[0] + count[1] - 3 + t))
                        ins = dve.scalar_tensor_tensor(prob0[:, a:a + w], prob1[:, a:a + w],
                                                       row_sum[:, 4 + t:5 + t], prob0[:, a:a + w],
                                                       ALU.mult, ALU.add)
                    ins.then_inc(p_ready, 1)
                if s == 7:
                    dve.wait_ge(bank_drained[1], i * 2 + 2 + BASE)
                    dve.wait_ge(bank_full[2], i * 2 + 2)
                    dve.tensor_tensor(prod[:, 2:T + 2], acc[:, 2, :], cc_f, ALU.mult
                                      ).then_inc(bank_drained[2], 1)
                    dve.wait_ge(bank_drained[2], i * 2 + 2 + BASE)
                    own(dve.tensor_scalar(mix[:, :], prod[:, 0:T], conv_col[:, bass.ds(i * 3, 1)], None,
                                          ALU.mult))
                    settle_hc()
                    for j in (1, 2):
                        own(dve.scalar_tensor_tensor(mix[:, :], prod[:, j:j + T],
                                                     conv_col[:, bass.ds(i * 3 + j, 1)], mix[:, :],
                                                     ALU.mult, ALU.add))
                        settle_hc()
                    dve.wait_ge(bank_drained[0], i * 2 + 2 + BASE)
                    own(dve.tensor_tensor(mix[:, :], mix[:, :], cb_f, ALU.mult))
                    dve.wait_ge(bank_drained[3], i * 2 + 2 + BASE)
                    own(dve.tensor_scalar(e_b[:, :], e_b[:, :], 1.0, None, ALU.add))
                    settle_hc()
                    own(dve.reciprocal(e_b[:, :], e_b[:, :]))
                    settle_hc()
                    own(dve.tensor_tensor(z_b[:, :], z_b[:, :], e_b[:, :], ALU.mult))
                    settle_hc()
                    dve.tensor_tensor(yb[:, bass.ds(i, 1), :].rearrange("p a t -> p (a t)"),
                                      mix[:, :], z_b[:, :], ALU.mult).then_inc(yb_done, 1)
                    dve.wait_ge(rms_ready, i + 1 + BASE)
                    own(dve.reciprocal(rms[:, :], rms[:, :]))
                    settle_hc()
                    own(dve.scalar_tensor_tensor(o_f[:, :], o_f[:, :], gain_col[:, 0:1], rms[:, :],
                                                 ALU.mult, ALU.mult))
                    settle_hc()
                    dve.tensor_tensor(ya[:, bass.ds(i, 1), :].rearrange("p a t -> p (a t)"),
                                      o_f[:, :], z_a[:, :], ALU.mult).then_inc(ya_done, 1)

            dve.wait_ge(bias_in, 16)
            rotate(0, settle)
            close(count[1])
            with dve.Fori(0, HEADS - 1) as i:
                for s in range(HC_HALVES):
                    lo_half(HEAD0, i, HC_HALVES, s + LEAD)
                    if s < 8:
                        attend_and_convolve(i, s, lambda: settle(i, HC_STEPS), i * HC_STEPS)
                rotate(i + 1, lambda: settle(i, HC_STEPS))
            close(HC_STEPS, HEADS - 1)
            for s in range(8):
                lo_half(HEAD0, HEADS - 1, HC_HALVES, s + LEAD)
                attend_and_convolve(HEADS - 1, s, settle, 0)
            close(count[1])

            def split_y(y, done, first):
                for k in range(HEADS):
                    own(dve.tensor_copy(y_hi[:, k, :], y[:, k, :]))
                for k in range(HEADS):
                    dve.wait_ge(step, count[0] + count[1] - HEADS + 1 + k)
                    dve.tensor_tensor(y_lo[:, k, :], y[:, k, :], y_hi[:, k, :].bitcast(F32), ALU.subtract
                                      ).then_inc(y_split, 1)

            dve.wait_ge(ya_done, HEADS + BASE)
            split_y(ya, ya_done, 0)
            close(HEADS)

            with dve.Fori(0, MERGES) as i:
                for s in range(MERGE_HALVES):
                    lo_half(A0, i, MERGE_HALVES, s + LEAD)
                for n in range(4):
                    if n < 3:
                        dve.wait_ge(bank_full[n], i * 2 + (A_BLOCK0 + 2))
                    else:
                        dve.wait_ge(half_done, i * MERGE_HALVES + (A0 + MERGE_HALVES + BASE))
                    dve.wait_ge(bank_drained[n], i * 2 + (A_BLOCK0 + 1 + BASE))
                    tile = h[:, bass.ds(i * 4 + n, 1), :].rearrange("p a t -> p (a t)")
                    dve.tensor_tensor(tile, acc[:, n, :], tile, ALU.mult).then_inc(bank_drained[n], 1)
            for n in range(4):
                dve.wait_ge(gate_reduced, 1)
                own(dve.tensor_scalar(gate[:, n * 512:(n + 1) * 512], misc[:, :] if n == 3 else sc[:, n, :],
                                      float(P), None, ALU.mult))
            dve.wait_ge(half_done, B0 + BASE)
            dve.wait_ge(yb_done, HEADS + BASE)
            split_y(yb, yb_done, HEADS)
            close(4 + HEADS)

            def h_lo(k):
                dve.wait_ge(h_hi_ready, k + 1)
                dve.tensor_tensor(act_lo[:, k, :], h[:, k, :], act_hi[:, k, :].bitcast(F32), ALU.subtract
                                  ).then_inc(h_split, 1)

            def merge_b(i, last=False):
                for s in range(MERGE_HALVES):
                    lo_half(B0, i, MERGE_HALVES, s + LEAD)
                    if last and s > 7:
                        for k in range(3 * (s - 8), 3 * (s - 8) + 3):
                            h_lo(k)
                for n in range(4):
                    if n < 3:
                        dve.wait_ge(bank_full[n], i * 2 + (B_BLOCK0 + 2))
                    else:
                        dve.wait_ge(half_done, i * MERGE_HALVES + (B0 + MERGE_HALVES + BASE))
                    dve.wait_ge(bank_drained[n], i * 2 + (B_BLOCK0 + 1 + BASE))
                    dve.tensor_tensor(sig_b[:, n, :], acc[:, n, :], sig_b[:, n, :], ALU.mult
                                      ).then_inc(bank_drained[n], 1)
                for n in range(4):
                    dve.wait_ge(bank_drained[n], i * 2 + (B_BLOCK0 + 2 + BASE))
                    tile = h[:, bass.ds(i * 4 + n, 1), :].rearrange("p a t -> p (a t)")
                    dve.tensor_tensor(tile, tile, sig_b[:, n, :], ALU.add).then_inc(h_ready, 1)

            with dve.Fori(0, MERGES - 1) as i:
                merge_b(i)
            merge_b(MERGES - 1, last=True)
            for k in range(KT - 4, KT):
                h_lo(k)

            OUT_STEPS = 2 * NT

            def residual(i, tiles, base):
                cols = bass.ds(i * COLS, COLS)
                for t in tiles:
                    if t < 3:
                        dve.wait_ge(bank_full[t], i + (O_BLOCK0 + 1))
                    else:
                        dve.wait_ge(half_done, i * OUT_HALVES + (O0 + OUT_HALVES + BASE))
                    dve.wait_ge(h_split, KT)
                    dve.tensor_tensor(res[:, t, cols], acc[:, t, :], gate[:, cols], ALU.mult
                                      ).then_inc(bank_drained[t], 1)
                dve.wait_ge(late_in, 48)
                for t in tiles:
                    dve.wait_ge(bank_drained[t], i + (O_BLOCK0 + 1 + BASE))
                    own(dve.scalar_tensor_tensor(res[:, t, cols], x_tok[:, t, cols], ALPHA,
                                                 res[:, t, cols], ALU.mult, ALU.add))
                for t in tiles:
                    dve.wait_ge(step, base + (count[0] + count[1] - (len(tiles) - 1)))
                    own(dve.bn_stats(stats[:, t, bass.ds(i, 1), :].rearrange("p a b -> p (a b)"),
                                     res[:, t, cols]))

            with dve.Fori(0, D // COLS - 1) as i:
                for s in range(OUT_HALVES):
                    lo_half(O0, i, OUT_HALVES, s + LEAD)
                residual(i, range(NT), i * OUT_STEPS)
            close(OUT_STEPS, D // COLS - 1)
            last = D // COLS - 1
            for s in range(OUT_HALVES - LEAD):
                lo_half(O0, last, OUT_HALVES, s + LEAD)
            for t in range(NT):
                residual(last, (t,), 0)
                settle()
                dve.bn_aggr(mean_var[:, t, :], stats[:, t, :, :]).then_inc(var_ready, 1)
                for n in range(2):
                    cols = slice(n * (D // 2), (n + 1) * (D // 2))
                    dve.wait_ge(var_ready, t + 1)
                    own(dve.scalar_tensor_tensor(res[:, t, cols], res[:, t, cols], mean_var[:, t, 0:1],
                                                 ln_g[:, cols], ALU.subtract, ALU.mult))
                dve.wait_ge(std_ready, t + 1)
                own(dve.reciprocal(rstd[:, t:t + 1], rstd[:, t:t + 1]))
                settle()
                for n in range(2):
                    cols = slice(n * (D // 2), (n + 1) * (D // 2))
                    dve.scalar_tensor_tensor(res[:, t, cols], res[:, t, cols], rstd[:, t:t + 1],
                                             ln_b[:, cols], ALU.mult, ALU.add).then_inc(y_ready, 1)

        @block.tensor
        def _(pe):
            def three(dst, a_hi, a_lo, b_hi, b_lo, first, last):
                pe.matmul(dst, a_hi, b_hi, start=first, stop=False)
                pe.matmul(dst, a_hi, b_lo, start=False, stop=False)
                return pe.matmul(dst, a_lo, b_hi, start=False, stop=last)

            def half(first, i, per, s, block0, blocks, at, n_halves, m_hi, m_lo, tokens=False):
                pe.wait_ge(lo_ready, i * per + (first + s + 1 + RAW_START))
                slot = s % SLOTS
                for n in range(4):
                    if at == 0:
                        pe.wait_ge(bank_drained[n], i * blocks + block0 + BASE)
                    for kk in range(2):
                        k = 2 * at + kk
                        cols = slice(n * P, (n + 1) * P)
                        ends = at == 0 and kk == 0, at == n_halves - 1 and kk == 1
                        if tokens:
                            ins = three(acc[:, n, :], m_hi[:, k, cols], m_lo[:, k, cols],
                                        w_hi[:, slot, kk, :], w_lo[:, slot, kk, :], *ends)
                        else:
                            ins = three(acc[:, n, :], w_hi[:, slot, kk, cols], w_lo[:, slot, kk, cols],
                                        m_hi[:, k, :], m_lo[:, k, :], *ends)
                    if n == 3:
                        ins.then_inc(half_done, 1)
                    elif at == n_halves - 1:
                        ins.then_inc(bank_full[n], 1)

            for events in (v_turned, o_done, p_turned, scores_done, half_done):
                pe.sem_inc(events, BASE)
            pe.wait_ge(small_in, 16 * SMALL)
            for g in range(GROUPS):
                pe.wait_ge(mod_step, (g + 1) * MOD_UNITS * MOD_STEPS + MOD_SLOTS * MOD_STEPS)
                for part in range(2):
                    for n in range(4):
                        at = 8 * g + 4 * part + n
                        ins = pe.matmul(misc[:, at:at + 1], mod_sum[:, g % 2, part, n * P:(n + 1) * P],
                                        one_col, start=True, stop=True)
                ins.then_inc(mod_reduced, 1)
                pe.wait_ge(u_lo_ready, 4 * g + 4)
                for s in (2 * g, 2 * g + 1):
                    half(0, 0, 0, s, 0, 0, s, 8, act_hi, act_lo)

            def attend(i, s):
                if s == 1:
                    pe.wait_ge(bank_drained[2], i * 2 + 1 + BASE)
                    pe.wait_ge(o_drained, i + BASE)
                    for t in range(NT):
                        ins = pe.transpose(misc[:, t * P:(t + 1) * P], v_f[:, t * P:(t + 1) * P], ident)
                    ins.then_inc(v_turned, 1)
                    pe.wait_ge(pt_ready, i + BASE)
                    pe.wait_ge(rms_ready, i + BASE)
                    pe.wait_ge(qk_ready, i * 2 + 2 + BASE)
                if s == 3:
                    pe.wait_ge(exp_done, i * 2 + 1)
                if s in (1, 3):
                    m = (s - 1) // 2
                    rows = slice(m * DH, (m + 1) * DH)
                    for t in range(NT):
                        b, c0 = SCORE_AT[t]
                        ins = pe.matmul(sc[:, b, c0:c0 + (t + 1) * P], q_f[rows, t * P:(t + 1) * P],
                                        k_f[rows, 0:(t + 1) * P], start=True, stop=True)
                    ins.then_inc(scores_done, 1)
                if s == 5:
                    pe.wait_ge(p_ready, i + 1 + BASE)
                    for j in range(NT):
                        b, c0 = SCORE_AT[3 - j]
                        for t in range(j, NT):
                            ins = pe.transpose(sc[:, b, c0 + (t - j) * P:c0 + (t - j + 1) * P],
                                               prob0[:, PROB_AT[t] + j * P:PROB_AT[t] + (j + 1) * P], ident)
                    ins.then_inc(p_turned, 1)
                if s == 6:
                    pe.wait_ge(v_ready, i + 1)
                    pe.wait_ge(pt_ready, i + 1 + BASE)
                    for j in range(NT):
                        a = PROB_AT[3 - j]
                        ins = pe.matmul(misc[:, j * P:T], v_tok[:, j * P:(j + 1) * P],
                                        prob_t[:, a:a + T - j * P], start=(j == 0), stop=(j == NT - 1))
                    ins.then_inc(o_done, 1)
                if s == 7:
                    pe.wait_ge(o_drained, i + 1 + BASE)
                    pe.matmul(sc[:, 2, :], mean_mat, o_sq[:, :], start=True, stop=True
                              ).then_inc(mean_done, 1)

            with pe.Fori(0, HEADS - 1) as i:
                for s in range(8):
                    half(HEAD0, i, HC_HALVES, s, 1, 2, s, 8, act_hi, act_lo)
                    attend(i, s)
                for s in range(8):
                    half(HEAD0, i, HC_HALVES, s + 8, 2, 2, s, 8, act_hi, act_lo)
            for s in range(8):
                half(HEAD0, HEADS - 1, HC_HALVES, s, 1, 2, s, 8, act_hi, act_lo)
                attend(HEADS - 1, s)

            for first, block0, n_split in ((A0, A_BLOCK0, HEADS), (B0, B_BLOCK0, 2 * HEADS)):
                with pe.Fori(0, MERGES) as i:
                    for s in range(8):
                        half(first, i, MERGE_HALVES, s, block0, 2, s, 8, act_hi, act_lo)
                    pe.wait_ge(y_split, n_split)
                    for s in range(8, 12):
                        half(first, i, MERGE_HALVES, s, block0 + 1, 2, s - 8, 4, y_hi, y_lo)
                if first == A0:
                    pe.wait_ge(gate_free, 4 * HEADS + 1)
                    pe.wait_ge(rms_ready, HEADS + BASE)
                    for n in range(4):
                        dst = misc[:, :] if n == 3 else sc[:, n, :]
                        ins = pe.matmul(dst, mean_mat, gate[:, n * 512:(n + 1) * 512], start=True, stop=True)
                    ins.then_inc(gate_reduced, 1)
            with pe.Fori(0, D // COLS - 1) as i:
                for s in range(OUT_HALVES):
                    pe.wait_ge(h_split, 2 * s + 2)
                    half(O0, i, OUT_HALVES, s, O_BLOCK0, 1, s, 8, act_hi, act_lo, tokens=True)
            last = D // COLS - 1
            for s in range(SLOTS):
                half(O0, last, OUT_HALVES, s, O_BLOCK0, 1, s, 8, act_hi, act_lo, tokens=True)
            for t in range(NT):
                for s in range(SLOTS, OUT_HALVES):
                    pe.wait_ge(lo_ready, O0 + last * OUT_HALVES + s + 1 + RAW_START)
                    for kk in range(2):
                        k = 2 * s + kk
                        cols = slice(t * P, (t + 1) * P)
                        ins = three(acc[:, t, :], act_hi[:, k, cols], act_lo[:, k, cols],
                                    w_hi[:, s % SLOTS, kk, :], w_lo[:, s % SLOTS, kk, :],
                                    False, s == OUT_HALVES - 1 and kk == 1)
                if t < 3:
                    ins.then_inc(bank_full[t], 1)
                else:
                    ins.then_inc(half_done, SLOTS)


def kernel(x, c, positions, w_mod, b_mod, w_in, lambda_q1, lambda_k1, lambda_q2, lambda_k2,
           subln_gain, conv_w, w_proj_a, w_proj_b, w_out, ln_gain, ln_bias):
    import concourse.bacc as bacc
    from concourse.bass_utils import run_bass_kernel_spmd

    a = np.asarray
    arrays = {
        "x": a(x)[0],
        "xT": a(x)[0].T,
        "cT": a(c)[0].reshape(KT, P).T,
        "positions": a(positions),
        "w_mod": a(w_mod)[0],
        "b_mod": a(b_mod),
        "b_cols": a(b_mod)[0].reshape(3 * KT, P).T[:, 0:2 * KT],
        "w_in": a(w_in)[0],
        "lams": np.concatenate([a(v) for v in (lambda_q1, lambda_k1, lambda_q2, lambda_k2)], axis=1),
        "gain": a(subln_gain).T,
        "conv_w": a(conv_w)[0].reshape(3, HEADS, P).transpose(2, 1, 0).reshape(P, 3 * HEADS),
        "w_tail": np.concatenate([a(w_out)[0], a(w_proj_a)[0], a(w_proj_b)[0]]),
        "ln_gain": a(ln_gain),
        "ln_bias": a(ln_bias),
        "consts": constants(),
    }
    nc = bacc.Bacc("TRN2", target_bir_lowering=False, num_devices=1)
    ins, sent = {}, {}
    for name, v in arrays.items():
        v = np.ascontiguousarray(v)
        sent[f"in_{name}"] = v
        ins[name] = nc.dram_tensor(f"in_{name}", v.shape, mybir.dt.from_np(v.dtype), kind="ExternalInput").ap()
    out = nc.dram_tensor("out", (T, D), F32, kind="ExternalOutput").ap()
    decoder_block(nc, out=out, **ins)
    r = run_bass_kernel_spmd(nc, [sent], core_ids=[0])
    return r.results[0]["out"].reshape(1, T, D)
```

```python
from contextlib import ExitStack

import numpy as np

import concourse.bass as bass
from concourse import mybir

F32 = mybir.dt.float32
F32R = mybir.dt.float32r
I32 = mybir.dt.int32
ALU = mybir.AluOpType
ACT = mybir.ActivationFunctionType
AX = mybir.AxisListType

P = 128
D = 2048
T = 512
KT = D // P
HEADS = 8
DH = 64
SEG = 1024
NT = T // P
COLS = 512
GATE_A, GATE_B = 8 * SEG, 8 * SEG + D
EPS = 1e-5
ALPHA = 2.0 ** 0.25
LAMBDA_INIT = 0.8 - 0.6
BIG = 3.0e38
RAW_START = 4
BASE = 1
GROUPS = 8
G_COLS = 2 * P
MOD_UNITS = 4
MOD_SLOTS = 4
MOD_STEPS = 4
V_COLS = (896, 896, 1024, 1600)
V_FIRST = tuple(c * 5 // 8 for c in V_COLS)
LEAD = 3
SLOTS = 4

HC_HALVES, HC_BLOCKS = 16, 2
MERGE_HALVES, MERGE_BLOCKS = 12, 2
OUT_HALVES, OUT_BLOCKS = 8, 1
MERGES = D // COLS
HEAD0 = GROUPS * 2 + 2
G_TILES = 3
A0, A_BLOCK0 = HEAD0 + HEADS * HC_HALVES - HC_HALVES // 2, HEADS * HC_BLOCKS
A_END0 = A0 + (MERGES - 1) * MERGE_HALVES
A_END_BLOCK = A_BLOCK0 + (MERGES - 1) * MERGE_BLOCKS
B0, B_BLOCK0 = A_END0 + 4, A_END_BLOCK + 1
O0, O_BLOCK0 = B0 + MERGES * MERGE_HALVES, B_BLOCK0 + MERGES * MERGE_BLOCKS
HALVES = O0 + (D // COLS) * OUT_HALVES

SCORE_AT = {3: (0, 0), 2: (1, 0), 0: (1, 384), 1: (2, 0)}
PROB_AT = {3: 0, 2: 512, 0: 896, 1: 1024}
PACKED = 1280

C_IDENT, C_MASK, C_FREQ, C_SIGN, C_WIDTH = 0, 128, 256, 257, 258


def constants():
    c = np.zeros((P, C_WIDTH), np.float32)
    c[:, C_IDENT:C_IDENT + P] = np.eye(P)
    q, k = np.meshgrid(np.arange(P), np.arange(P), indexing="ij")
    c[:, C_MASK:C_MASK + P] = np.where(k <= q, BIG, -BIG)
    freq = (10000.0 ** (-np.arange(0, DH, 2) / DH)).astype(np.float32)
    c[:, C_FREQ] = np.tile(freq, 4)
    c[:, C_SIGN] = np.where((np.arange(P) // 32) % 2 == 0, -1.0, 1.0)
    return c


def decoder_block(nc, x, xT, cT, positions, w_mod, b_mod, b_cols, w_in, lams, gain, conv_w, w_tail,
                  ln_gain, ln_bias, consts, out):
    ctx = ExitStack()
    with ctx:
        def sb(name, shape, dt=F32, scope=None):
            return (scope or ctx).enter_context(nc.sbuf_tensor(name, shape, dt))

        def sem(name):
            return ctx.enter_context(nc.semaphore(name))

        raw = sb("raw", [P, 2, 4, COLS])
        w_hi = sb("w_hi", [P, SLOTS, 2, COLS], F32R)
        w_lo = sb("w_lo", [P, SLOTS, 2, COLS], F32R)
        act_hi = sb("act_hi", [P, KT, T], F32R)
        act_lo = sb("act_lo", [P, KT, T], F32R)
        gate = sb("gate", [P, D])
        cst = sb("cst", [P, C_WIDTH])
        cos = sb("cos", [P, T])
        sin = sb("sin", [P, T])
        c_col = sb("c_col", [P, KT])
        b_col = sb("b_col", [P, 2 * KT])
        conv_col = sb("conv_col", [P, HEADS * 3])
        gain_col = sb("gain_col", [P, 1])
        eps_col = sb("eps_col", [P, 1])
        one_col = sb("one_col", [P, 1])
        mean_mat = sb("mean_mat", [P, P], F32R)
        mod = sb("mod", [P, 2 * KT])
        lam_dot = sb("lam_dot", [P, 2])
        lam_exp = sb("lam_exp", [P, 2])
        neg_lam = sb("neg_lam", [P, 1])
        row_max = sb("row_max", [P, 4])
        neg_max = sb("neg_max", [P, 8])
        row_sum = sb("row_sum", [P, 8])
        stats = sb("stats", [P, NT, D // COLS, 6])
        mean_var = sb("mean_var", [P, NT, 2])
        rstd = sb("rstd", [P, NT])
        shift_col = sb("shift_col", [P, NT])

        def stage(name_shapes):
            scope = ExitStack()
            made = [sb(n, s, d, scope) for n, s, d in name_shapes]
            scope.close()
            return made

        with ExitStack() as place:
            mod_sum = sb("mod_sum", [P, 2, 2, 2, G_COLS], F32, place)
            lam_in = sb("lam_in", [P, 4, DH], F32, place)
            place.close()
        with ExitStack() as place:
            sig_b = sb("sig_b", [P, 4, T], F32, place)
            place.close()
        ln_g, ln_b = stage([("ln_g", [P, D], F32), ("ln_b", [P, D], F32)])
        yb = sb("yb", [P, HEADS, T])
        x_in, w_mod_in = stage([("x_in", [P, KT, T], F32),
                                ("w_mod_in", [P, MOD_SLOTS, MOD_STEPS, 2, G_COLS], F32)])
        (sig_a, ya, gate_in, q_raw, q_rot, k_raw, k_rot, v_f, v_tok, z_a, e_a, prob0, prob1,
         prob_t, o_f, prod, mix) = stage([
            ("sig_a", [P, 4, T], F32), ("ya", [P, HEADS, T], F32), ("gate_in", [P, D // 2], F32),
            ("q_raw", [P, T], F32), ("q_rot", [P, T], F32), ("k_raw", [P, T], F32),
            ("k_rot", [P, T], F32),
            ("v_f", [P, T], F32), ("v_tok", [P, T], F32), ("z_a", [P, T], F32),
            ("e_a", [P, T], F32), ("prob0", [P, PACKED], F32), ("prob1", [P, PACKED], F32),
            ("prob_t", [P, PACKED], F32), ("o_f", [P, T], F32), ("prod", [P, T + 2], F32),
            ("mix", [P, T], F32)])
        q_f, k_f = prob_t[:, 0:T], prob_t[:, T:2 * T]
        _, sq_hi, sq_lo = stage([("before_sq", [P, (4 + HEADS) * T + D // 2 + 8 * T + 2 * PACKED], F32),
                                 ("sq_hi", [P, T], F32R), ("sq_lo", [P, T], F32R)])
        cb_f, cc_f = prob1[:, 0:T], prob1[:, T:2 * T]
        z_b, e_b, o_sq, rms = q_raw, q_rot, k_raw, k_rot
        h, y_hi, y_lo = stage([("h", [P, KT, T], F32), ("y_hi", [P, HEADS, T], F32R),
                               ("y_lo", [P, HEADS, T], F32R)])
        res, x_tok = stage([("res", [P, NT, D], F32), ("x_tok", [P, NT, D], F32)])

        acc = ctx.enter_context(nc.psum_tensor("acc", [P, 4, COLS], F32))
        sc = ctx.enter_context(nc.psum_tensor("sc", [P, 3, 512], F32))
        misc = ctx.enter_context(nc.psum_tensor("misc", [P, 512], F32))

        ident = cst[:, C_IDENT:C_IDENT + P]
        mask = cst[:, C_MASK:C_MASK + P]

        b_in = sem("b_in")
        small_in = sem("small_in")
        ones_set = sem("ones_set")
        c_in = sem("c_in")
        x_landed = [sem("x_landed0"), sem("x_landed1")]
        bias_in = sem("bias_in")
        sums_clear = sem("sums_clear")
        mod_landed = [sem(f"mod_landed{s}") for s in range(4)]
        mod_step = sem("mod_step")
        sum_clear = sem("sum_clear")
        mod_reduced = sem("mod_reduced")
        mod_ready = sem("mod_ready")
        lam_sem = sem("lam_sem")
        trig_ready = sem("trig_ready")
        sin_done = sem("sin_done")
        u_ready = sem("u_ready")
        u_lo_ready = sem("u_lo_ready")
        raw_landed = [sem("raw_landed0"), sem("raw_landed1")]
        hi_ready = sem("hi_ready")
        lo_ready = sem("lo_ready")
        half_done = sem("half_done")
        bank_full = [sem(f"bank_full{n}") for n in range(3)]
        bank_drained = [sem(f"bank_drained{n}") for n in range(4)]
        gate_landed = sem("gate_landed")
        gate_free = sem("gate_free")
        gate_reduced = sem("gate_reduced")
        gate_ready = sem("gate_ready")
        qk_swapped = sem("qk_swapped")
        qk_ready = sem("qk_ready")
        v_turned = sem("v_turned")
        v_ready = sem("v_ready")
        scores_done = sem("scores_done")
        max_ready = sem("max_ready")
        exp_done = sem("exp_done")
        p_ready = sem("p_ready")
        p_turned = sem("p_turned")
        pt_ready = sem("pt_ready")
        o_done = sem("o_done")
        o_drained = sem("o_drained")
        sq_split = sem("sq_split")
        mean_done = sem("mean_done")
        rms_ready = sem("rms_ready")
        ya_done = sem("ya_done")
        yb_done = sem("yb_done")
        y_split = sem("y_split")
        h_ready = sem("h_ready")
        h_hi_ready = sem("h_hi_ready")
        h_split = sem("h_split")
        late_in = sem("late_in")
        step = sem("step")
        var_ready = sem("var_ready")
        std_ready = sem("std_ready")
        norm_ready = sem("norm_ready")
        normed = sem("normed")
        pool_step = sem("pool_step")
        pool_ready = sem("pool_ready")
        y_ready = sem("y_ready")
        stored = sem("stored")

        SMALL = 5
        block = ctx.enter_context(nc.Block())

        @block.gpsimd
        def _(pool):
            for g in range(GROUPS):
                if g >= 2:
                    pool.wait_ge(mod_reduced, g - 1)
                pool.memset(mod_sum[:, g % 2], 0.0).then_inc(sum_clear, 1)
            pool.wait_ge(u_lo_ready, KT)
            with pool.Fori(0, HEADS) as i:
                for m in range(4):
                    pool.wait_ge(gate_free, i * 4 + (m + 1))
                    pool.dma_start(gate_in[:, :],
                                   w_mod[bass.ds(i * (2 * P) + (m // 2) * P, P),
                                         2 * D + (m % 2) * (D // 2):2 * D + (m % 2 + 1) * (D // 2)]
                                   ).then_inc(gate_landed, 16)
            for t in range(NT):
                tail = res[:, t, V_COLS[t]:D]
                pool.wait_ge(normed, t + 1)
                pool.tensor_tensor(tail, tail, ln_g[:, V_COLS[t]:D], ALU.mult).then_inc(pool_step, 1)
                pool.wait_ge(pool_step, t + 1)
                pool.tensor_tensor(tail, tail, ln_b[:, V_COLS[t]:D], ALU.add).then_inc(pool_ready, 1)

        @block.sync
        def _(sp):
            sp.dma_start(c_col[:, :], cT).then_inc(c_in, 16)
            sp.dma_start(b_col[:, :], b_cols).then_inc(b_in, 16)
            def wait_raw(i, per, u):
                sp.wait_ge(lo_ready, i * (2 * per) + (2 * (u - 1) + RAW_START))

            def head_unit(s, col, raw_slot):
                rows = w_in[s * 4 * P:(s + 1) * 4 * P, 0:4 * SEG]
                quarter(rows, col, raw_slot)

            def conv_unit(s, col, raw_slot):
                rows = w_in[s * 4 * P:(s + 1) * 4 * P, 4 * SEG:8 * SEG]
                quarter(rows, col, raw_slot)

            def quarter(rows, col, raw_slot, tiles=4):
                view = rows.rearrange("(k p) (g c) -> p k g c", p=P, g=4)
                for k in range(tiles):
                    sp.dma_start(raw[:, raw_slot, k, :].rearrange("p (g c) -> p g c", g=4),
                                 view[:, k, :, bass.ds(col, P)]).then_inc(raw_landed[raw_slot], 16)

            for g in range(GROUPS):
                for n in range(MOD_UNITS):
                    unit = g * MOD_UNITS + n
                    if unit >= MOD_SLOTS:
                        sp.wait_ge(mod_step, (unit + 1) * MOD_STEPS)
                    for part, first_col in enumerate((D, 0)):
                        cols = slice(first_col + g * G_COLS, first_col + (g + 1) * G_COLS)
                        rows = w_mod[n * MOD_STEPS * P:(n + 1) * MOD_STEPS * P, cols]
                        sp.dma_start(w_mod_in[:, unit % MOD_SLOTS, :, part, :],
                                     rows.rearrange("(k p) c -> p k c", p=P)
                                     ).then_inc(mod_landed[unit % MOD_SLOTS], 16)
                    if n == 1:
                        sp.dma_start(x_in[:, 2 * g:2 * g + 2, :],
                                     xT[g * 2 * P:(g + 1) * 2 * P, :].rearrange("(k p) t -> p k t", p=P)
                                     ).then_inc(x_landed[g % 2], 16)
                if g >= 2:
                    wait_raw(0, 0, g)
                rows = w_in[g * 2 * P:(g + 1) * 2 * P, :]
                quarter(rows[:, 0:4 * SEG], 0, g % 2, 2)
                sp.dma_start(raw[:, g % 2, 2:4, 0:G_TILES * P],
                             rows[:, GATE_A:GATE_A + G_TILES * P].rearrange("(k p) c -> p k c", p=P)
                             ).then_inc(raw_landed[g % 2], 32)
            sp.dma_start(cst[:, :], consts).then_inc(small_in, 16)
            sp.dma_start(sin[:, :].bitcast(I32), positions.broadcast_to([P, T])).then_inc(small_in, 16)
            sp.dma_start(conv_col[:, :], conv_w).then_inc(small_in, 16)
            sp.dma_start(gain_col[:, :], gain).then_inc(small_in, 16)
            sp.dma_start(lam_in[:, :, :].rearrange("p a d -> p (a d)"),
                         lams.broadcast_to([P, 4 * DH])).then_inc(small_in, 16)
            wait_raw(0, 0, GROUPS)
            sp.dma_start(raw[:, 0, :, :].rearrange("p a (b c) -> p (a b) c", c=P),
                         w_in[:, GATE_A + G_TILES * P:GATE_A + (G_TILES + 1) * P].rearrange(
                             "(k p) c -> p k c", p=P)).then_inc(raw_landed[0], 64)

            with sp.Fori(0, HEADS - 1) as i:
                for s in range(8):
                    unit = HEAD0 // 2 + s
                    wait_raw(i, 8, unit)
                    if s < 4:
                        conv_unit(s, i * P, unit % 2)
                    else:
                        head_unit(s - 4, i * P + P, unit % 2)
            for s in range(4):
                unit = HEAD0 // 2 + s
                wait_raw(HEADS - 1, 8, unit)
                conv_unit(s, (HEADS - 1) * P, unit % 2)

            def plain_unit(w, r, col, i, per, unit):
                wait_raw(i, per, unit)
                sp.dma_start(raw[:, unit % 2], w[r * 4 * P:(r + 1) * 4 * P, bass.ds(col, COLS)].rearrange(
                    "(k p) c -> p k c", p=P)).then_inc(raw_landed[unit % 2], 64)

            with sp.Fori(0, MERGES - 1) as i:
                for s in range(4):
                    plain_unit(w_in, s, i * COLS + (GATE_A + COLS), i, 6, A0 // 2 + s)
                for s in (4, 5):
                    plain_unit(w_tail, s, i * COLS + COLS, i, 6, A0 // 2 + s)
            for s in range(2):
                plain_unit(w_tail, 4 + s, 0, 0, 0, A_END0 // 2 + s)
            with sp.Fori(0, MERGES) as i:
                for s in range(4):
                    plain_unit(w_in, s, i * COLS + GATE_B, i, 6, B0 // 2 + s)
                for s in (4, 5):
                    plain_unit(w_tail, s + 2, i * COLS, i, 6, B0 // 2 + s)
            with sp.Fori(0, D // COLS) as i:
                for s in range(4):
                    plain_unit(w_tail, s, i * COLS, i, 4, O0 // 2 + s)
            for t in range(NT):
                for n in range(2):
                    cols = slice(n * V_FIRST[t], V_COLS[t] if n else V_FIRST[t])
                    sp.wait_ge(y_ready, 2 * t + n + 1)
                    sp.dma_start(out[t * P:(t + 1) * P, cols], res[:, t, cols]).then_inc(stored, 16)
                if t < NT - 1:
                    sp.wait_ge(pool_ready, t + 1)
                    sp.dma_start(out[t * P:(t + 1) * P, V_COLS[t]:D], res[:, t, V_COLS[t]:D]
                                 ).then_inc(stored, 16)
            sp.wait_ge(stored, 16 * 3 * NT)

        @block.scalar
        def _(act):
            def copy(dst, src):
                return act.activation(dst, src, ACT.Copy)

            def round_raw(f, i, per):
                unit = f // 2
                act.wait_ge(raw_landed[unit % 2], i * (16 * per) + 64 * (unit // 2 + 1))
                width = G_TILES * P if f < 2 * GROUPS and f % 2 else COLS
                copy(w_hi[:, f % SLOTS, :, 0:width],
                     raw[:, unit % 2, 2 * (f % 2):2 * (f % 2) + 2, 0:width]).then_inc(hi_ready, 1)

            def round_at(first, i, per, s):
                act.wait_ge(half_done, i * per + (first + s - LEAD + BASE))
                round_raw(first + s, i, per)

            def drain_head(i, z_done):
                for n, (plain, turned) in enumerate(((q_raw, q_rot), (k_raw, k_rot))):
                    act.wait_ge(bank_full[n], i * 2 + 1)
                    act.wait_ge(qk_ready, i * 2 + BASE)
                    act.wait_ge(yb_done, i + BASE)
                    act.wait_ge(ya_done, i + BASE)
                    copy(plain[:, :], acc[:, n, :]).then_inc(bank_drained[n], 1)
                act.wait_ge(bank_full[2], i * 2 + 1)
                act.wait_ge(v_turned, i + BASE)
                copy(v_f[:, :], acc[:, 2, :]).then_inc(bank_drained[2], 1)
                act.wait_ge(half_done, z_done)
                copy(z_a[:, :], acc[:, 3, :])
                act.activation(e_a[:, :], acc[:, 3, :], ACT.Exp, scale=-1.0
                               ).then_inc(bank_drained[3], 1)
                for n, (plain, turned) in enumerate(((q_raw, q_rot), (k_raw, k_rot))):
                    act.wait_ge(bank_drained[n], i * 2 + 1 + BASE)
                    for g in range(4):
                        to = g ^ 1
                        ins = copy(turned[32 * to:32 * to + 32, :], plain[32 * g:32 * g + 32, :])
                    ins.then_inc(qk_swapped, 1)

            act.sem_inc(rms_ready, BASE)
            for g in range(GROUPS):
                act.wait_ge(mod_ready, g + 1)
                act.wait_ge(x_landed[g % 2], 16 * (g // 2 + 1))
                for k in (2 * g, 2 * g + 1):
                    act.activation(act_hi[:, k, :], x_in[:, k, :], ACT.Identity,
                                   scale=mod[:, KT + k:KT + k + 1], bias=mod[:, k:k + 1]
                                   ).then_inc(u_ready, 1)
                for f in (2 * g, 2 * g + 1):
                    if f < SLOTS:
                        round_raw(f, 0, 0)
                    else:
                        round_at(f, 0, 0, 0)
            round_at(HEAD0, 0, 0, -2)
            round_at(HEAD0, 0, 0, -1)
            drain_head(0, HEAD0 - 3 + BASE)
            round_at(HEAD0, 0, 0, 0)
            act.wait_ge(lam_sem, 1)
            act.activation(lam_exp[:, :], lam_dot[:, :], ACT.Exp).then_inc(lam_sem, 1)
            for n, table in enumerate((cos, sin)):
                act.wait_ge(trig_ready, n + 1)
                act.activation(table[:, :], table[:, :], ACT.Sin).then_inc(sin_done, 1)
            act.wait_ge(sums_clear, 1)
            act.dma_start(gate[0:1, :], b_mod[0:1, 2 * D:3 * D]).then_inc(bias_in, 16)

            def attend_and_convolve(i, s):
                if s == 2:
                    act.wait_ge(v_turned, i + 1 + BASE)
                    act.wait_ge(o_done, i + BASE)
                    copy(v_tok[:, :], misc[:, :]).then_inc(v_ready, 1)
                if s in (2, 4):
                    m = (s - 2) // 2
                    act.wait_ge(max_ready, i * 2 + (m + 1))
                    act.wait_ge(p_ready if m else p_turned, i + BASE)
                    prob = prob1 if m else prob0
                    for t in (3, 2, 0, 1):
                        b, c0 = SCORE_AT[t]
                        w = (t + 1) * P
                        e = act.activation(prob[:, PROB_AT[t]:PROB_AT[t] + w], sc[:, b, c0:c0 + w],
                                           ACT.Exp, bias=neg_max[:, 4 * m + t:4 * m + t + 1],
                                           scale=DH ** -0.5,
                                           accum_out=row_sum[:, 4 * m + t:4 * m + t + 1])
                    e.then_inc(exp_done, 1)
                if s == 6:
                    act.wait_ge(p_turned, i + 1 + BASE)
                    act.wait_ge(o_done, i + BASE)
                    copy(prob_t[:, 0:512], sc[:, 0, :])
                    copy(prob_t[:, 512:1024], sc[:, 1, :])
                    copy(prob_t[:, 1024:1280], sc[:, 2, 0:256]).then_inc(pt_ready, 1)
                if s == 7:
                    act.wait_ge(o_done, i + 1 + BASE)
                    act.wait_ge(ya_done, i + BASE)
                    copy(o_f[:, :], misc[:, :])
                    act.activation(sq_hi[:, :], misc[:, :], ACT.Square)
                    act.activation(o_sq[:, :], misc[:, :], ACT.Square).then_inc(o_drained, 1)
                    act.wait_ge(bank_full[0], i * 2 + 2)
                    act.wait_ge(yb_done, i + BASE)
                    copy(cb_f, acc[:, 0, :]).then_inc(bank_drained[0], 1)
                    act.wait_ge(bank_full[1], i * 2 + 2)
                    copy(cc_f, acc[:, 1, :]).then_inc(bank_drained[1], 1)
                    act.wait_ge(half_done, i * HC_HALVES + (HEAD0 + 8 + BASE))
                    copy(z_b[:, :], acc[:, 3, :])
                    act.activation(e_b[:, :], acc[:, 3, :], ACT.Exp, scale=-1.0
                                   ).then_inc(bank_drained[3], 1)
                    act.wait_ge(mean_done, i + 1)
                    act.activation(rms[:, :], sc[:, 2, :], ACT.Sqrt, bias=eps_col[:, 0:1]
                                   ).then_inc(rms_ready, 1)

            act.wait_ge(half_done, HEAD0 - 2 + BASE)
            for n in range(G_TILES):
                ins = act.activation(sig_a[:, n, :], sc[:, n, :], ACT.Sigmoid)
            ins.then_inc(pt_ready, 1)
            for s in range(1, LEAD):
                round_at(HEAD0, 0, 0, s)
            act.wait_ge(half_done, HEAD0 + BASE)
            act.activation(sig_a[:, G_TILES, :], misc[:, :], ACT.Sigmoid).then_inc(o_drained, 1)
            with act.Fori(0, HEADS - 1) as i:
                for s in range(HC_HALVES):
                    round_at(HEAD0, i, HC_HALVES, s + LEAD)
                    if s < 8:
                        attend_and_convolve(i, s)
                drain_head(i + 1, i * HC_HALVES + (HEAD0 + HC_HALVES + BASE))
            for s in range(8):
                round_at(HEAD0, HEADS - 1, HC_HALVES, s + LEAD)
                attend_and_convolve(HEADS - 1, s)

            with act.Fori(0, MERGES - 1) as i:
                for s in range(MERGE_HALVES):
                    round_at(A0, i, MERGE_HALVES, s + LEAD)
                    if s == 7:
                        for n in range(4):
                            if n < 3:
                                act.wait_ge(bank_full[n], i * 2 + (A_BLOCK0 + 1))
                            else:
                                act.wait_ge(half_done, i * MERGE_HALVES + (A0 + 8 + BASE))
                            act.wait_ge(y_split, HEADS)
                            act.activation(h[:, bass.ds(i * 4 + (4 + n), 1), :].rearrange("p a t -> p (a t)"),
                                           acc[:, n, :], ACT.Sigmoid).then_inc(bank_drained[n], 1)
            for s in range(4):
                round_at(A_END0, 0, 0, s + LEAD)
            def merge_b(i, last=False):
                for s in range(MERGE_HALVES):
                    round_at(B0, i, MERGE_HALVES, s + LEAD)
                    if s == 7:
                        act.wait_ge(y_split, 2 * HEADS)
                        for n in range(4):
                            act.wait_ge(h_ready, i * 4 + BASE)
                            if n < 3:
                                act.wait_ge(bank_full[n], i * 2 + (B_BLOCK0 + 1))
                            else:
                                act.wait_ge(half_done, i * MERGE_HALVES + (B0 + 8 + BASE))
                            act.activation(sig_b[:, n, :], acc[:, n, :], ACT.Sigmoid
                                           ).then_inc(bank_drained[n], 1)
                    if last and s > 7:
                        act.wait_ge(half_done, O0 - 4 + BASE)
                        for k in range(3 * (s - 8), 3 * (s - 8) + 3):
                            copy(act_hi[:, k, :], h[:, k, :]).then_inc(h_hi_ready, 1)

            with act.Fori(0, MERGES - 1) as i:
                merge_b(i)
            merge_b(MERGES - 1, last=True)
            for k in range(KT - 4, KT):
                act.wait_ge(h_ready, k + 1 + BASE)
                copy(act_hi[:, k, :], h[:, k, :]).then_inc(h_hi_ready, 1)
            act.wait_ge(half_done, O0 + BASE)
            act.wait_ge(h_ready, KT + BASE)
            act.dma_start(x_tok[:, :, :], x.rearrange("(t p) d -> p t d", p=P)).then_inc(late_in, 16)
            act.dma_start(ln_g[:, :], ln_gain.broadcast_to([P, D])).then_inc(late_in, 16)
            act.dma_start(ln_b[:, :], ln_bias.broadcast_to([P, D])).then_inc(late_in, 16)
            with act.Fori(0, D // COLS - 1) as i:
                for s in range(OUT_HALVES):
                    round_at(O0, i, OUT_HALVES, s + LEAD)
            for s in range(OUT_HALVES - LEAD):
                round_at(O0, D // COLS - 1, OUT_HALVES, s + LEAD)
            for t in range(NT):
                act.wait_ge(var_ready, t + 1)
                act.activation(rstd[:, t:t + 1], mean_var[:, t, 1:2], ACT.Sqrt, bias=eps_col[:, 0:1]
                               ).then_inc(std_ready, 1)
                act.wait_ge(norm_ready, t + 1)
                act.activation(res[:, t, V_COLS[t]:D], res[:, t, V_COLS[t]:D], ACT.Identity,
                               scale=rstd[:, t:t + 1], bias=shift_col[:, t:t + 1]).then_inc(normed, 1)
            act.wait_ge(pool_ready, NT)
            act.dma_start(out[(NT - 1) * P:T, V_COLS[-1]:D], res[:, NT - 1, V_COLS[-1]:D]
                          ).then_inc(stored, 16)

        @block.vector
        def _(dve):
            count = [0, 0]

            def own(ins):
                ins.then_inc(step, 1)
                count[1] += 1

            def settle(i=0, per=0):
                dve.wait_ge(step, i * per + (count[0] + count[1]))

            def close(per, times=1):
                assert per == count[1], (per, count)
                count[0] += per * times
                count[1] = 0

            def lo_half(first, i, per, s):
                dve.wait_ge(hi_ready, i * per + (first + s + 1))
                f = first + s
                width = G_TILES * P if f < 2 * GROUPS and f % 2 else COLS
                ins = dve.tensor_tensor(w_lo[:, f % SLOTS, :, 0:width],
                                        raw[:, (f // 2) % 2, 2 * (f % 2):2 * (f % 2) + 2, 0:width],
                                        w_hi[:, f % SLOTS, :, 0:width].bitcast(F32), ALU.subtract)
                ins.then_inc(lo_ready, 1)

            for events in (qk_ready, ya_done, yb_done, p_ready, h_ready, *bank_drained):
                dve.sem_inc(events, BASE)
            dve.sem_inc(lo_ready, RAW_START)
            dve.sem_inc(mod_step, MOD_SLOTS * MOD_STEPS)
            dve.sem_inc(gate_free, 1)
            own(dve.memset(eps_col[:, :], EPS))
            dve.memset(one_col[:, :], 1.0).then_inc(ones_set, 1)
            dve.wait_ge(c_in, 16)

            def sum_unit(unit):
                g, n = divmod(unit, MOD_UNITS)
                dve.wait_ge(mod_landed[unit % MOD_SLOTS], 32 * (unit // MOD_SLOTS + 1))
                for a in range(MOD_STEPS):
                    e = MOD_STEPS * unit + a
                    dst = mod_sum[:, g % 2, a % 2].rearrange("p a c -> p (a c)")
                    if e % (MOD_UNITS * MOD_STEPS) >= 2:
                        dve.wait_ge(mod_step, e - 1 + MOD_SLOTS * MOD_STEPS)
                    else:
                        dve.wait_ge(sum_clear, g + 1)
                    dve.scalar_tensor_tensor(dst,
                                             w_mod_in[:, unit % MOD_SLOTS, a].rearrange("p a c -> p (a c)"),
                                             c_col[:, MOD_STEPS * n + a:MOD_STEPS * n + a + 1], dst,
                                             ALU.mult, ALU.add).then_inc(mod_step, 1)

            def columns(g):
                dve.wait_ge(b_in, 16)
                dve.wait_ge(mod_reduced, g + 1)
                two = slice(2 * g, 2 * g + 2)
                own(dve.tensor_tensor(mod[:, two], misc[:, 4 * g + 2:4 * g + 4], b_col[:, two], ALU.add))
                dve.scalar_tensor_tensor(mod[:, KT + 2 * g:KT + 2 * g + 2], misc[:, 4 * g:4 * g + 2], 1.0,
                                         b_col[:, KT + 2 * g:KT + 2 * g + 2], ALU.add, ALU.add
                                         ).then_inc(mod_ready, 1)

            def u_lo(g):
                dve.wait_ge(x_landed[g % 2], 16 * (g // 2 + 1))
                dve.wait_ge(mod_ready, g + 1)
                settle()
                full = {k: gate[:, (k % 2) * T:(k % 2 + 1) * T] for k in (2 * g, 2 * g + 1)}
                for k in full:
                    own(dve.tensor_scalar(full[k], x_in[:, k, :], mod[:, KT + k:KT + k + 1],
                                          mod[:, k:k + 1], ALU.mult, ALU.add))
                settle()
                for k in full:
                    dve.wait_ge(u_ready, k + 1)
                    dve.tensor_tensor(act_lo[:, k, :], full[k], act_hi[:, k, :].bitcast(F32),
                                      ALU.subtract).then_inc(u_lo_ready, 1)

            def lambda_dots():
                own(dve.tensor_tensor(lam_in[:, 0, :], lam_in[:, 0, :], lam_in[:, 1, :], ALU.mult))
                own(dve.tensor_tensor(lam_in[:, 2, :], lam_in[:, 2, :], lam_in[:, 3, :], ALU.mult))
                settle()
                own(dve.tensor_reduce(lam_dot[:, 0:1], lam_in[:, 0, :], AX.X, ALU.add))
                dve.tensor_reduce(lam_dot[:, 1:2], lam_in[:, 2, :], AX.X, ALU.add).then_inc(lam_sem, 1)

            ang, turns = gate[:, 0:T], gate[:, T:2 * T]

            def angles():
                own(dve.tensor_copy(ang, sin[:, :].bitcast(I32)))
                settle()
                own(dve.tensor_scalar(ang, ang, cst[:, C_FREQ:C_FREQ + 1], None, ALU.mult))
                settle()

            def bring_down(table, shift):
                two_pi = (6.28125, 1.9340515136718750e-03, 1.2556659146447340e-06)
                magic = 1.5 * 2.0 ** 23
                own(dve.tensor_scalar(turns, ang, 1.0 / (2 * np.pi), shift, ALU.mult, ALU.add))
                settle()
                own(dve.tensor_scalar(turns, turns, magic, magic, ALU.add, ALU.subtract))
                settle()
                own(dve.scalar_tensor_tensor(table[:, :], turns, -two_pi[0], ang, ALU.mult, ALU.add))
                settle()
                for part in two_pi[1:]:
                    own(dve.scalar_tensor_tensor(table[:, :], turns, -part, table[:, :], ALU.mult, ALU.add))
                    settle()
                own(dve.tensor_scalar(table[:, :], table[:, :], shift * 2 * np.pi, 3.1415925, ALU.add, ALU.min))
                settle()
                dve.tensor_scalar(table[:, :], table[:, :], -3.1415925, None, ALU.max).then_inc(trig_ready, 1)

            for g in range(GROUPS):
                for n in range(MOD_UNITS):
                    sum_unit(g * MOD_UNITS + n)
                    if g and n == 0:
                        columns(g - 1)
                    if g and n == 1:
                        u_lo(g - 1)
                        lo_half(2 * (g - 1), 0, 0, 0)
                    if g and n == 2:
                        lo_half(2 * (g - 1), 0, 0, 1)
            columns(GROUPS - 1)
            u_lo(GROUPS - 1)
            for s in range(-4, 0):
                lo_half(HEAD0, 0, 0, s)
            dve.wait_ge(small_in, 16 * SMALL)
            lambda_dots()
            own(dve.memset(cos[:, 0:P], 1.0 / P))
            settle()
            own(dve.tensor_copy(mean_mat[:, :], cos[:, 0:P]))
            settle()
            angles()
            bring_down(cos, 0.25)
            lo_half(HEAD0, 0, 0, 0)
            bring_down(sin, 0.0)
            dve.memset(gate[:, :], 0.0).then_inc(sums_clear, 1)
            for s in range(1, LEAD):
                lo_half(HEAD0, 0, 0, s)
            dve.wait_ge(lam_sem, 2)
            own(dve.tensor_scalar(neg_lam[:, :], lam_exp[:, 1:2], -LAMBDA_INIT, None, ALU.add))
            settle()
            own(dve.tensor_tensor(neg_lam[:, :], neg_lam[:, :], lam_exp[:, 0:1], ALU.subtract))
            own(dve.tensor_scalar(gain_col[:, :], gain_col[:, :], 1.0 - LAMBDA_INIT, None, ALU.mult))
            dve.wait_ge(sin_done, 2)
            own(dve.tensor_scalar(sin[:, :], sin[:, :], cst[:, C_SIGN:C_SIGN + 1], None, ALU.mult))
            dve.wait_ge(u_lo_ready, KT)
            own(dve.memset(prod[:, 0:2], 0.0))
            settle()

            HC_STEPS = 26

            def rotate(i, settle_hc):
                dve.wait_ge(o_done, i + BASE)
                for n, (plain, turned, dst) in enumerate(((q_raw, q_rot, q_f), (k_raw, k_rot, k_f))):
                    dve.wait_ge(qk_swapped, i * 2 + n + 1)
                    own(dve.tensor_tensor(plain[:, :], plain[:, :], cos[:, :], ALU.mult))
                    own(dve.tensor_tensor(turned[:, :], turned[:, :], sin[:, :], ALU.mult))
                    settle_hc()
                    dve.tensor_tensor(dst[:, :], plain[:, :], turned[:, :], ALU.add).then_inc(qk_ready, 1)
                dve.wait_ge(bank_drained[3], i * 2 + 1 + BASE)
                own(dve.tensor_scalar(e_a[:, :], e_a[:, :], 1.0, None, ALU.add))
                settle_hc()
                own(dve.reciprocal(e_a[:, :], e_a[:, :]))
                settle_hc()
                own(dve.tensor_tensor(z_a[:, :], z_a[:, :], e_a[:, :], ALU.mult))

            def attend_and_convolve(i, s, settle_hc, base):
                if s % 2 == 1:
                    m = s // 2
                    dst = gate[:, (m % 2) * (D // 2):(m % 2 + 1) * (D // 2)]
                    dve.wait_ge(gate_landed, i * 64 + 16 * (m + 1))
                    dve.wait_ge(gate_free, i * 4 + (m + 1))
                    dve.scalar_tensor_tensor(dst, gate_in[:, :], c_col[:, bass.ds(i * 2 + m // 2, 1)],
                                             dst, ALU.mult, ALU.add).then_inc(gate_free, 1)
                if s in (2, 4):
                    m = (s - 2) // 2
                    dve.wait_ge(scores_done, i * 2 + (m + 1 + BASE))
                    for t in range(NT):
                        b, c0 = SCORE_AT[t]
                        edge = sc[:, b, c0 + t * P:c0 + (t + 1) * P]
                        ins = dve.tensor_tensor(edge, edge, mask, ALU.min)
                    own(ins)
                    settle_hc()
                    for t in range(NT):
                        b, c0 = SCORE_AT[t]
                        ins = dve.tensor_reduce(row_max[:, t:t + 1], sc[:, b, c0:c0 + (t + 1) * P],
                                                AX.X, ALU.max)
                    own(ins)
                    settle_hc()
                    dve.tensor_scalar(neg_max[:, 4 * m:4 * m + 4], row_max[:, :], -DH ** -0.5, None,
                                      ALU.mult).then_inc(max_ready, 1)
                if s == 4:
                    dve.wait_ge(exp_done, i * 2 + 2)
                    own(dve.reciprocal(row_sum[:, :], row_sum[:, :]))
                    settle_hc()
                    own(dve.tensor_scalar(row_sum[:, 4:8], row_sum[:, 4:8], neg_lam[:, 0:1], None, ALU.mult))
                    settle_hc()
                    for t in range(NT):
                        a, w = PROB_AT[t], (t + 1) * P
                        own(dve.tensor_scalar(prob0[:, a:a + w], prob0[:, a:a + w], row_sum[:, t:t + 1],
                                              None, ALU.mult))
                    for t in range(NT):
                        a, w = PROB_AT[t], (t + 1) * P
                        dve.wait_ge(step, base + (count[0] + count[1] - 3 + t))
                        ins = dve.scalar_tensor_tensor(prob0[:, a:a + w], prob1[:, a:a + w],
                                                       row_sum[:, 4 + t:5 + t], prob0[:, a:a + w],
                                                       ALU.mult, ALU.add)
                    ins.then_inc(p_ready, 1)
                if s == 7:
                    dve.wait_ge(o_drained, i + 1 + BASE)
                    dve.tensor_tensor(sq_lo[:, :], o_sq[:, :], sq_hi[:, :].bitcast(F32), ALU.subtract
                                      ).then_inc(sq_split, 1)
                    dve.wait_ge(bank_drained[1], i * 2 + 2 + BASE)
                    dve.wait_ge(bank_full[2], i * 2 + 2)
                    dve.tensor_tensor(prod[:, 2:T + 2], acc[:, 2, :], cc_f, ALU.mult
                                      ).then_inc(bank_drained[2], 1)
                    dve.wait_ge(bank_drained[2], i * 2 + 2 + BASE)
                    own(dve.tensor_scalar(mix[:, :], prod[:, 0:T], conv_col[:, bass.ds(i * 3, 1)], None,
                                          ALU.mult))
                    settle_hc()
                    for j in (1, 2):
                        own(dve.scalar_tensor_tensor(mix[:, :], prod[:, j:j + T],
                                                     conv_col[:, bass.ds(i * 3 + j, 1)], mix[:, :],
                                                     ALU.mult, ALU.add))
                        settle_hc()
                    dve.wait_ge(bank_drained[0], i * 2 + 2 + BASE)
                    own(dve.tensor_tensor(mix[:, :], mix[:, :], cb_f, ALU.mult))
                    dve.wait_ge(bank_drained[3], i * 2 + 2 + BASE)
                    own(dve.tensor_scalar(e_b[:, :], e_b[:, :], 1.0, None, ALU.add))
                    settle_hc()
                    own(dve.reciprocal(e_b[:, :], e_b[:, :]))
                    settle_hc()
                    own(dve.tensor_tensor(z_b[:, :], z_b[:, :], e_b[:, :], ALU.mult))
                    settle_hc()
                    dve.tensor_tensor(yb[:, bass.ds(i, 1), :].rearrange("p a t -> p (a t)"),
                                      mix[:, :], z_b[:, :], ALU.mult).then_inc(yb_done, 1)
                    dve.wait_ge(rms_ready, i + 1 + BASE)
                    own(dve.reciprocal(rms[:, :], rms[:, :]))
                    settle_hc()
                    own(dve.scalar_tensor_tensor(o_f[:, :], o_f[:, :], gain_col[:, 0:1], rms[:, :],
                                                 ALU.mult, ALU.mult))
                    settle_hc()
                    dve.tensor_tensor(ya[:, bass.ds(i, 1), :].rearrange("p a t -> p (a t)"),
                                      o_f[:, :], z_a[:, :], ALU.mult).then_inc(ya_done, 1)

            dve.wait_ge(bias_in, 16)
            rotate(0, settle)
            close(count[1])
            with dve.Fori(0, HEADS - 1) as i:
                for s in range(HC_HALVES):
                    lo_half(HEAD0, i, HC_HALVES, s + LEAD)
                    if s < 8:
                        attend_and_convolve(i, s, lambda: settle(i, HC_STEPS), i * HC_STEPS)
                rotate(i + 1, lambda: settle(i, HC_STEPS))
            close(HC_STEPS, HEADS - 1)
            for s in range(8):
                lo_half(HEAD0, HEADS - 1, HC_HALVES, s + LEAD)
                attend_and_convolve(HEADS - 1, s, settle, 0)
            close(count[1])

            def split_y(y):
                for k in range(HEADS):
                    own(dve.tensor_copy(y_hi[:, k, :], y[:, k, :]))
                for k in range(HEADS):
                    dve.wait_ge(step, count[0] + count[1] - HEADS + 1 + k)
                    dve.tensor_tensor(y_lo[:, k, :], y[:, k, :], y_hi[:, k, :].bitcast(F32), ALU.subtract
                                      ).then_inc(y_split, 1)

            def gate_a(first_tile, full, full3, sigmoids=None):
                for n in range(4):
                    if n < 3:
                        dve.wait_ge(bank_full[n], full)
                    else:
                        dve.wait_ge(half_done, full3)
                    if sigmoids is not None:
                        dve.wait_ge(bank_drained[n], sigmoids)
                    tile = h[:, bass.ds(first_tile + n, 1), :].rearrange("p a t -> p (a t)")
                    dve.tensor_tensor(tile, acc[:, n, :], tile if sigmoids is not None else sig_a[:, n, :],
                                      ALU.mult).then_inc(bank_drained[n], 1)

            for s in range(2):
                lo_half(A0, 0, 0, s + LEAD)
            dve.wait_ge(ya_done, HEADS + BASE)
            split_y(ya)
            close(HEADS)
            for s in range(2, MERGE_HALVES):
                lo_half(A0, 0, 0, s + LEAD)
            gate_a(4, A_BLOCK0 + 2, A0 + MERGE_HALVES + BASE, A_BLOCK0 + 1 + BASE)
            with dve.Fori(1, MERGES - 1) as i:
                for s in range(MERGE_HALVES):
                    lo_half(A0, i, MERGE_HALVES, s + LEAD)
                gate_a(i * 4 + 4, i * 2 + (A_BLOCK0 + 2), i * MERGE_HALVES + (A0 + MERGE_HALVES + BASE),
                       i * 2 + (A_BLOCK0 + 1 + BASE))
            for s in range(4):
                lo_half(A_END0, 0, 0, s + LEAD)
            gate_a(0, B_BLOCK0, B0 + BASE)
            for n in range(4):
                dve.wait_ge(gate_reduced, 1)
                own(dve.tensor_scalar(gate[:, n * 512:(n + 1) * 512], misc[:, :] if n == 3 else sc[:, n, :],
                                      float(P), None, ALU.mult))
            dve.wait_ge(half_done, B0 + BASE)
            dve.wait_ge(yb_done, HEADS + BASE)
            split_y(yb)
            close(4 + HEADS)

            def h_lo(k):
                dve.wait_ge(h_hi_ready, k + 1)
                dve.tensor_tensor(act_lo[:, k, :], h[:, k, :], act_hi[:, k, :].bitcast(F32), ALU.subtract
                                  ).then_inc(h_split, 1)

            def merge_b(i, last=False):
                for s in range(MERGE_HALVES):
                    lo_half(B0, i, MERGE_HALVES, s + LEAD)
                    if last and s > 7:
                        for k in range(3 * (s - 8), 3 * (s - 8) + 3):
                            h_lo(k)
                for n in range(4):
                    if n < 3:
                        dve.wait_ge(bank_full[n], i * 2 + (B_BLOCK0 + 2))
                    else:
                        dve.wait_ge(half_done, i * MERGE_HALVES + (B0 + MERGE_HALVES + BASE))
                    dve.wait_ge(bank_drained[n], i * 2 + (B_BLOCK0 + 1 + BASE))
                    dve.tensor_tensor(sig_b[:, n, :], acc[:, n, :], sig_b[:, n, :], ALU.mult
                                      ).then_inc(bank_drained[n], 1)
                for n in range(4):
                    dve.wait_ge(bank_drained[n], i * 2 + (B_BLOCK0 + 2 + BASE))
                    tile = h[:, bass.ds(i * 4 + n, 1), :].rearrange("p a t -> p (a t)")
                    dve.tensor_tensor(tile, tile, sig_b[:, n, :], ALU.add).then_inc(h_ready, 1)

            with dve.Fori(0, MERGES - 1) as i:
                merge_b(i)
            merge_b(MERGES - 1, last=True)
            for k in range(KT - 4, KT):
                h_lo(k)

            OUT_STEPS = 2 * NT

            def residual(i, tiles, base):
                cols = bass.ds(i * COLS, COLS)
                for t in tiles:
                    if t < 3:
                        dve.wait_ge(bank_full[t], i + (O_BLOCK0 + 1))
                    else:
                        dve.wait_ge(half_done, i * OUT_HALVES + (O0 + OUT_HALVES + BASE))
                    dve.wait_ge(h_split, KT)
                    dve.tensor_tensor(res[:, t, cols], acc[:, t, :], gate[:, cols], ALU.mult
                                      ).then_inc(bank_drained[t], 1)
                dve.wait_ge(late_in, 48)
                for t in tiles:
                    dve.wait_ge(bank_drained[t], i + (O_BLOCK0 + 1 + BASE))
                    own(dve.scalar_tensor_tensor(res[:, t, cols], x_tok[:, t, cols], ALPHA,
                                                 res[:, t, cols], ALU.mult, ALU.add))
                for t in tiles:
                    dve.wait_ge(step, base + (count[0] + count[1] - (len(tiles) - 1)))
                    own(dve.bn_stats(stats[:, t, bass.ds(i, 1), :].rearrange("p a b -> p (a b)"),
                                     res[:, t, cols]))

            with dve.Fori(0, D // COLS - 1) as i:
                for s in range(OUT_HALVES):
                    lo_half(O0, i, OUT_HALVES, s + LEAD)
                residual(i, range(NT), i * OUT_STEPS)
            close(OUT_STEPS, D // COLS - 1)
            last = D // COLS - 1
            for s in range(OUT_HALVES - LEAD):
                lo_half(O0, last, OUT_HALVES, s + LEAD)
            for t in range(NT):
                residual(last, (t,), 0)
                settle()
                dve.bn_aggr(mean_var[:, t, :], stats[:, t, :, :]).then_inc(var_ready, 1)
                for n in range(2):
                    cols = slice(n * V_FIRST[t], V_COLS[t] if n else V_FIRST[t])
                    dve.wait_ge(var_ready, t + 1)
                    own(dve.scalar_tensor_tensor(res[:, t, cols], res[:, t, cols], mean_var[:, t, 0:1],
                                                 ln_g[:, cols], ALU.subtract, ALU.mult))
                dve.wait_ge(std_ready, t + 1)
                own(dve.reciprocal(rstd[:, t:t + 1], rstd[:, t:t + 1]))
                settle()
                dve.tensor_scalar(shift_col[:, t:t + 1], mean_var[:, t, 0:1], rstd[:, t:t + 1], -1.0,
                                  ALU.mult, ALU.mult).then_inc(norm_ready, 1)
                for n in range(2):
                    cols = slice(n * V_FIRST[t], V_COLS[t] if n else V_FIRST[t])
                    dve.scalar_tensor_tensor(res[:, t, cols], res[:, t, cols], rstd[:, t:t + 1],
                                             ln_b[:, cols], ALU.mult, ALU.add).then_inc(y_ready, 1)

        @block.tensor
        def _(pe):
            def three(dst, a_hi, a_lo, b_hi, b_lo, first, last):
                pe.matmul(dst, a_hi, b_hi, start=first, stop=False)
                pe.matmul(dst, a_hi, b_lo, start=False, stop=False)
                return pe.matmul(dst, a_lo, b_hi, start=False, stop=last)

            def half(first, i, per, s, block0, blocks, at, n_halves, m_hi, m_lo, tokens=False):
                pe.wait_ge(lo_ready, i * per + (first + s + 1 + RAW_START))
                slot = (first + s) % SLOTS
                for n in range(4):
                    if at == 0:
                        pe.wait_ge(bank_drained[n], i * blocks + block0 + BASE)
                    for kk in range(2):
                        k = 2 * at + kk
                        cols = slice(n * P, (n + 1) * P)
                        ends = at == 0 and kk == 0, at == n_halves - 1 and kk == 1
                        if tokens:
                            ins = three(acc[:, n, :], m_hi[:, k, cols], m_lo[:, k, cols],
                                        w_hi[:, slot, kk, :], w_lo[:, slot, kk, :], *ends)
                        else:
                            ins = three(acc[:, n, :], w_hi[:, slot, kk, cols], w_lo[:, slot, kk, cols],
                                        m_hi[:, k, :], m_lo[:, k, :], *ends)
                    if n == 3:
                        ins.then_inc(half_done, 1)
                    elif at == n_halves - 1:
                        ins.then_inc(bank_full[n], 1)

            def gate_half(g):
                f = 2 * g + 1
                pe.wait_ge(lo_ready, f + 1 + RAW_START)
                for n in range(G_TILES):
                    cols = slice(n * P, (n + 1) * P)
                    for kk in range(2):
                        k = 2 * g + kk
                        ins = three(sc[:, n, :], w_hi[:, f % SLOTS, kk, cols], w_lo[:, f % SLOTS, kk, cols],
                                    act_hi[:, k, :], act_lo[:, k, :], k == 0, k == KT - 1)
                ins.then_inc(half_done, 1)

            for events in (v_turned, o_done, p_turned, scores_done, half_done):
                pe.sem_inc(events, BASE)
            pe.wait_ge(ones_set, 1)
            for g in range(GROUPS):
                pe.wait_ge(mod_step, (g + 1) * MOD_UNITS * MOD_STEPS + MOD_SLOTS * MOD_STEPS)
                for part in range(2):
                    for n in range(2):
                        at = 4 * g + 2 * part + n
                        for a in range(2):
                            ins = pe.matmul(misc[:, at:at + 1], mod_sum[:, g % 2, a, part, n * P:(n + 1) * P],
                                            one_col[:, :], start=(a == 0), stop=(a == 1))
                ins.then_inc(mod_reduced, 1)
                if g:
                    gate_half(g - 1)
                pe.wait_ge(u_lo_ready, 2 * g + 2)
                half(0, 0, 0, 2 * g, 0, 0, g, 8, act_hi, act_lo)
            gate_half(GROUPS - 1)
            for a in range(2):
                f = HEAD0 - 2 + a
                pe.wait_ge(lo_ready, f + 1 + RAW_START)
                tile_hi = w_hi[:, f % SLOTS].rearrange("p a (b c) -> p (a b) c", c=P)
                tile_lo = w_lo[:, f % SLOTS].rearrange("p a (b c) -> p (a b) c", c=P)
                for kk in range(8):
                    k = 8 * a + kk
                    ins = three(misc[:, :], tile_hi[:, kk, :], tile_lo[:, kk, :],
                                act_hi[:, k, :], act_lo[:, k, :], k == 0, k == KT - 1)
                ins.then_inc(half_done, 1)

            def attend(i, s):
                if s == 1:
                    pe.wait_ge(bank_drained[2], i * 2 + 1 + BASE)
                    pe.wait_ge(o_drained, i + BASE)
                    for t in range(NT):
                        ins = pe.transpose(misc[:, t * P:(t + 1) * P], v_f[:, t * P:(t + 1) * P], ident)
                    ins.then_inc(v_turned, 1)
                    pe.wait_ge(pt_ready, i + BASE)
                    pe.wait_ge(rms_ready, i + BASE)
                    pe.wait_ge(qk_ready, i * 2 + 2 + BASE)
                if s == 3:
                    pe.wait_ge(exp_done, i * 2 + 1)
                if s in (1, 3):
                    m = (s - 1) // 2
                    rows = slice(m * DH, (m + 1) * DH)
                    for t in range(NT):
                        b, c0 = SCORE_AT[t]
                        ins = pe.matmul(sc[:, b, c0:c0 + (t + 1) * P], q_f[rows, t * P:(t + 1) * P],
                                        k_f[rows, 0:(t + 1) * P], start=True, stop=True)
                    ins.then_inc(scores_done, 1)
                if s == 5:
                    pe.wait_ge(p_ready, i + 1 + BASE)
                    for j in range(NT):
                        b, c0 = SCORE_AT[3 - j]
                        for t in range(j, NT):
                            ins = pe.transpose(sc[:, b, c0 + (t - j) * P:c0 + (t - j + 1) * P],
                                               prob0[:, PROB_AT[t] + j * P:PROB_AT[t] + (j + 1) * P], ident)
                    ins.then_inc(p_turned, 1)
                if s == 6:
                    pe.wait_ge(v_ready, i + 1)
                    pe.wait_ge(pt_ready, i + 1 + BASE)
                    for j in range(NT):
                        a = PROB_AT[3 - j]
                        ins = pe.matmul(misc[:, j * P:T], v_tok[:, j * P:(j + 1) * P],
                                        prob_t[:, a:a + T - j * P], start=(j == 0), stop=(j == NT - 1))
                    ins.then_inc(o_done, 1)
                if s == 7:
                    pe.wait_ge(sq_split, i + 1)
                    pe.matmul(sc[:, 2, :], mean_mat[:, :], sq_hi[:, :], start=True, stop=False)
                    pe.matmul(sc[:, 2, :], mean_mat[:, :], sq_lo[:, :], start=False, stop=True
                              ).then_inc(mean_done, 1)

            with pe.Fori(0, HEADS - 1) as i:
                for s in range(8):
                    half(HEAD0, i, HC_HALVES, s, 1, 2, s, 8, act_hi, act_lo)
                    attend(i, s)
                for s in range(8):
                    half(HEAD0, i, HC_HALVES, s + 8, 2, 2, s, 8, act_hi, act_lo)
            for s in range(8):
                half(HEAD0, HEADS - 1, HC_HALVES, s, 1, 2, s, 8, act_hi, act_lo)
                attend(HEADS - 1, s)

            for first, block0, n_split, times in ((A0, A_BLOCK0, HEADS, MERGES - 1),
                                                  (B0, B_BLOCK0, 2 * HEADS, MERGES)):
                with pe.Fori(0, times) as i:
                    for s in range(8):
                        half(first, i, MERGE_HALVES, s, block0, 2, s, 8, act_hi, act_lo)
                    pe.wait_ge(y_split, n_split)
                    for s in range(8, 12):
                        half(first, i, MERGE_HALVES, s, block0 + 1, 2, s - 8, 4, y_hi, y_lo)
                if first == A0:
                    for s in range(4):
                        half(A_END0, 0, 0, s, A_END_BLOCK, 0, s, 4, y_hi, y_lo)
                    pe.wait_ge(gate_free, 4 * HEADS + 1)
                    pe.wait_ge(rms_ready, HEADS + BASE)
                    for n in range(4):
                        dst = misc[:, :] if n == 3 else sc[:, n, :]
                        ins = pe.matmul(dst, mean_mat[:, :].bitcast(F32), gate[:, n * 512:(n + 1) * 512],
                                        start=True, stop=True)
                    ins.then_inc(gate_reduced, 1)
            with pe.Fori(0, D // COLS - 1) as i:
                for s in range(OUT_HALVES):
                    pe.wait_ge(h_split, 2 * s + 2)
                    half(O0, i, OUT_HALVES, s, O_BLOCK0, 1, s, 8, act_hi, act_lo, tokens=True)
            last = D // COLS - 1
            for s in range(SLOTS):
                half(O0, last, OUT_HALVES, s, O_BLOCK0, 1, s, 8, act_hi, act_lo, tokens=True)
            for t in range(NT):
                for s in range(SLOTS, OUT_HALVES):
                    pe.wait_ge(lo_ready, O0 + last * OUT_HALVES + s + 1 + RAW_START)
                    for kk in range(2):
                        k = 2 * s + kk
                        cols = slice(t * P, (t + 1) * P)
                        ins = three(acc[:, t, :], act_hi[:, k, cols], act_lo[:, k, cols],
                                    w_hi[:, (O0 + s) % SLOTS, kk, :], w_lo[:, (O0 + s) % SLOTS, kk, :],
                                    False, s == OUT_HALVES - 1 and kk == 1)
                if t < 3:
                    ins.then_inc(bank_full[t], 1)
                else:
                    ins.then_inc(half_done, SLOTS)


def kernel(x, c, positions, w_mod, b_mod, w_in, lambda_q1, lambda_k1, lambda_q2, lambda_k2,
           subln_gain, conv_w, w_proj_a, w_proj_b, w_out, ln_gain, ln_bias):
    import concourse.bacc as bacc
    from concourse.bass_utils import run_bass_kernel_spmd

    a = np.asarray
    arrays = {
        "x": a(x)[0],
        "xT": a(x)[0].T,
        "cT": a(c)[0].reshape(KT, P).T,
        "positions": a(positions),
        "w_mod": a(w_mod)[0],
        "b_mod": a(b_mod),
        "b_cols": a(b_mod)[0].reshape(3 * KT, P).T[:, 0:2 * KT],
        "w_in": a(w_in)[0],
        "lams": np.concatenate([a(v) for v in (lambda_q1, lambda_k1, lambda_q2, lambda_k2)], axis=1),
        "gain": a(subln_gain).T,
        "conv_w": a(conv_w)[0].reshape(3, HEADS, P).transpose(2, 1, 0).reshape(P, 3 * HEADS),
        "w_tail": np.concatenate([a(w_out)[0], a(w_proj_a)[0], a(w_proj_b)[0]]),
        "ln_gain": a(ln_gain),
        "ln_bias": a(ln_bias),
        "consts": constants(),
    }
    nc = bacc.Bacc("TRN2", target_bir_lowering=False, num_devices=1)
    ins, sent = {}, {}
    for name, v in arrays.items():
        v = np.ascontiguousarray(v)
        sent[f"in_{name}"] = v
        ins[name] = nc.dram_tensor(f"in_{name}", v.shape, mybir.dt.from_np(v.dtype), kind="ExternalInput").ap()
    out = nc.dram_tensor("out", (T, D), F32, kind="ExternalOutput").ap()
    decoder_block(nc, out=out, **ins)
    r = run_bass_kernel_spmd(nc, [sent], core_ids=[0])
    return r.results[0]["out"].reshape(1, T, D)
```
